# Optimizing a Trainium2 kernel written in Bass

```python
import math
import jax
import jax.numpy as jnp
from jax import lax
import numpy as np

D_MODEL = 1024
BATCH = 1
SEQ = 256
DEPTH = 1

MEM_LEN = 256
NORM_EPS = 1e-5
QK_EPS = 1e-6

SSM_WIDTH = D_MODEL // 2
SSM_GROUP = 16
SSM_GROUPS = SSM_WIDTH // SSM_GROUP
SSM_STATE = 64
SSM_DT_MIN = 0.001
SSM_DT_MAX = 0.1

HEAD_DIM = 64
SWA_Q_HEADS = D_MODEL // HEAD_DIM
SWA_KV_HEADS = 4
SWA_GROUP = SWA_Q_HEADS // SWA_KV_HEADS
WINDOW = 128
BLOCK = 128
ROPE_THETA = 500000.0
ROPE_DIM = HEAD_DIM // 4

MEM_HEADS = 4
MEM_HEAD_DIM = 128

SWA_Q_WIDTH = SWA_Q_HEADS * HEAD_DIM
SWA_KV_WIDTH = SWA_KV_HEADS * HEAD_DIM
MEM_WIDTH = MEM_HEADS * MEM_HEAD_DIM
N_BRANCH = 3
IN_WIDTHS = (SSM_WIDTH, SWA_Q_WIDTH, SWA_KV_WIDTH, SWA_KV_WIDTH, MEM_WIDTH, N_BRANCH * D_MODEL)
IN_WIDTH = sum(IN_WIDTHS)

N_EXPERTS = 32
TOP_K = 4
D_EXPERT = D_MODEL
SWIGLU_ALPHA = 1.702
SWIGLU_LIMIT = 7.0

kernel_name = 'hybrid_gated_s5_swa_mem_moe'

def rmsnorm(x, g, eps):
    xf = x.astype(jnp.float32)
    y = xf * lax.rsqrt(jnp.mean(xf * xf, axis=-1, keepdims=True) + eps)
    return (y * g.astype(jnp.float32)).astype(x.dtype)

def partial_rope(t, positions):
    half = ROPE_DIM // 2
    inv_freq = ROPE_THETA ** (-jnp.arange(half, dtype=jnp.float32) / half)
    ang = positions.astype(jnp.float32)[..., None] * inv_freq
    cos = jnp.cos(ang)[:, :, None, :]
    sin = jnp.sin(ang)[:, :, None, :]
    tr = t[..., :ROPE_DIM].astype(jnp.float32)
    t1, t2 = tr[..., :half], tr[..., half:]
    rot = jnp.concatenate([t1 * cos - t2 * sin, t2 * cos + t1 * sin], axis=-1).astype(t.dtype)
    return jnp.concatenate([rot, t[..., ROPE_DIM:]], axis=-1)

def s5_branch(u, log_dt, a_re, a_im, b_re, b_im, c_re, c_im, d_skip, w_glu_v, w_glu_g):
    f32 = jnp.float32
    bsz, seq, _ = u.shape
    dt = jnp.exp(log_dt.astype(f32))[:, None]
    lam = lax.complex(jnp.minimum(a_re.astype(f32), -1e-4), a_im.astype(f32))
    a_bar = jnp.exp(lam * dt)
    b = lax.complex(b_re.astype(f32), b_im.astype(f32))
    b_bar = ((a_bar - 1.0) / lam)[..., None] * b
    c = lax.complex(c_re.astype(f32), c_im.astype(f32))
    uf = u.astype(f32)
    ug = uf.reshape(bsz, seq, SSM_GROUPS, SSM_GROUP).astype(jnp.complex64)
    bu = jnp.einsum('bsgc,gpc->bsgp', ug, b_bar)
    a_elems = jnp.broadcast_to(a_bar[None, None], (1, seq, SSM_GROUPS, SSM_STATE))

    def combine(left, right):
        a_l, b_l = left
        a_r, b_r = right
        return a_r * a_l, a_r * b_l + b_r

    _, states = lax.associative_scan(combine, (a_elems, bu), axis=1)
    y = jnp.einsum('bsgp,gcp->bsgc', states, c).real.reshape(bsz, seq, SSM_WIDTH)
    y = y + d_skip.astype(f32) * uf
    y = jax.nn.gelu(y).astype(u.dtype)
    return (y @ w_glu_v) * jax.nn.sigmoid(y @ w_glu_g)

def swa_branch(q, k, v, positions, q_gain, k_gain, sinks):
    f32 = jnp.float32
    bsz, seq = q.shape[0], q.shape[1]
    nb = seq // BLOCK
    q = partial_rope(rmsnorm(q, q_gain, QK_EPS), positions)
    k = partial_rope(rmsnorm(k, k_gain, QK_EPS), positions)
    qb = q.reshape(bsz, nb, BLOCK, SWA_KV_HEADS, SWA_GROUP, HEAD_DIM)

    def with_prev(t):
        tb = t.reshape(bsz, nb, BLOCK, SWA_KV_HEADS, HEAD_DIM)
        prev = jnp.pad(tb[:, :-1], ((0, 0), (1, 0), (0, 0), (0, 0), (0, 0)))
        return jnp.concatenate([prev, tb], axis=2)

    kb, vb = with_prev(k), with_prev(v)
    scores = jnp.einsum('bnqhgd,bnkhd->bnhgqk', qb, kb, preferred_element_type=f32) * (HEAD_DIM ** -0.5)
    qi = jnp.arange(BLOCK)[:, None]
    ki = jnp.arange(2 * BLOCK)[None, :] - BLOCK
    rel = qi - ki
    band = (rel >= 0) & (rel < WINDOW)
    valid = band[None] & ((jnp.arange(nb)[:, None, None] > 0) | (ki[None] >= 0))
    scores = jnp.where(valid[None, :, None, None], scores, -jnp.inf)
    sink = sinks.astype(f32).reshape(SWA_KV_HEADS, SWA_GROUP)[None, None, :, :, None, None]
    m = jnp.maximum(jnp.max(scores, axis=-1, keepdims=True), sink)
    p = jnp.exp(scores - m)
    p = p / (jnp.sum(p, axis=-1, keepdims=True) + jnp.exp(sink - m))
    out = jnp.einsum('bnhgqk,bnkhd->bnqhgd', p.astype(v.dtype), vb)
    return out.reshape(bsz, seq, SWA_Q_WIDTH)

def mem_branch(q, mk, mv, q_gain, k_gain):
    bsz, seq = q.shape[0], q.shape[1]
    q = rmsnorm(q, q_gain, QK_EPS)
    mk = rmsnorm(mk, k_gain, QK_EPS)
    s = jnp.einsum('bshd,bmhd->bhsm', q, mk, preferred_element_type=jnp.float32) * (MEM_HEAD_DIM ** -0.5)
    p = jax.nn.softmax(s, axis=-1)
    out = jnp.einsum('bhsm,bmhd->bshd', p.astype(mv.dtype), mv)
    return out.reshape(bsz, seq, MEM_WIDTH)

def moe_ffn(h, w_router, b_router, w1, b1, w2, b2):
    f32 = jnp.float32
    bsz, seq, d = h.shape
    t = h.reshape(-1, d)
    logits = (t @ w_router + b_router).astype(f32)
    top_vals, top_idx = lax.top_k(logits, TOP_K)
    top_w = jax.nn.softmax(top_vals, axis=-1)
    comb = jnp.sum(jax.nn.one_hot(top_idx, N_EXPERTS, dtype=f32) * top_w[..., None], axis=1)
    out = jnp.zeros((t.shape[0], d), f32)
    for e in range(N_EXPERTS):
        hid = t @ w1[e] + b1[e]
        x_glu = jnp.minimum(hid[:, ::2], SWIGLU_LIMIT)
        x_lin = jnp.clip(hid[:, 1::2], -SWIGLU_LIMIT, SWIGLU_LIMIT)
        act = x_glu * jax.nn.sigmoid(SWIGLU_ALPHA * x_glu) * (x_lin + 1.0)
        y = act @ w2[e] + b2[e]
        out = out + comb[:, e:e + 1] * y.astype(f32)
    return out.astype(h.dtype).reshape(bsz, seq, d)

def setup_inputs(seed: int = 0) -> dict:
    key = jax.random.key(seed)
    ks = jax.random.split(key, 40)
    f32 = jnp.float32
    L = DEPTH

    def nrm(k, shape, scale):
        return jax.random.normal(k, shape, f32) * scale

    def gain(k, n):
        return 1.0 + 0.02 * jax.random.normal(k, (L, n), f32)

    x = nrm(ks[0], (BATCH, SEQ, D_MODEL), 1.0)
    mem = nrm(ks[1], (BATCH, MEM_LEN, D_MODEL), 1.0)
    offset = jax.random.randint(ks[2], (BATCH, 1), 0, 4096, dtype=jnp.int32)
    positions = offset + jnp.arange(SEQ, dtype=jnp.int32)[None, :]
    n_idx = jnp.arange(SSM_STATE, dtype=f32)
    return {
        'x': x,
        'mem': mem,
        'positions': positions,
        'attn_norm_g': gain(ks[3], D_MODEL),
        'mem_norm_g': gain(ks[4], D_MODEL),
        'w_in': nrm(ks[5], (L, D_MODEL, IN_WIDTH), D_MODEL ** -0.5),
        'b_gate': nrm(ks[6], (L, N_BRANCH * D_MODEL), 0.02),
        'ssm_log_dt': jax.random.uniform(ks[7], (L, SSM_GROUPS), f32, math.log(SSM_DT_MIN), math.log(SSM_DT_MAX)),
        'ssm_a_re': -0.5 + nrm(ks[8], (L, SSM_GROUPS, SSM_STATE), 0.01),
        'ssm_a_im': jnp.pi * n_idx + nrm(ks[9], (L, SSM_GROUPS, SSM_STATE), 0.01),
        'ssm_b_re': nrm(ks[10], (L, SSM_GROUPS, SSM_STATE, SSM_GROUP), (2.0 * SSM_GROUP) ** -0.5),
        'ssm_b_im': nrm(ks[11], (L, SSM_GROUPS, SSM_STATE, SSM_GROUP), (2.0 * SSM_GROUP) ** -0.5),
        'ssm_c_re': nrm(ks[12], (L, SSM_GROUPS, SSM_GROUP, SSM_STATE), (2.0 * SSM_STATE) ** -0.5),
        'ssm_c_im': nrm(ks[13], (L, SSM_GROUPS, SSM_GROUP, SSM_STATE), (2.0 * SSM_STATE) ** -0.5),
        'ssm_d': nrm(ks[14], (L, SSM_WIDTH), 1.0),
        'w_glu_v': nrm(ks[15], (L, SSM_WIDTH, SSM_WIDTH), SSM_WIDTH ** -0.5),
        'w_glu_g': nrm(ks[16], (L, SSM_WIDTH, SSM_WIDTH), SSM_WIDTH ** -0.5),
        'swa_q_gain': gain(ks[17], HEAD_DIM),
        'swa_k_gain': gain(ks[18], HEAD_DIM),
        'swa_sinks': nrm(ks[19], (L, SWA_Q_HEADS), 0.5),
        'w_mem_kv': nrm(ks[20], (L, D_MODEL, 2 * MEM_WIDTH), D_MODEL ** -0.5),
        'mem_q_gain': gain(ks[21], MEM_HEAD_DIM),
        'mem_k_gain': gain(ks[22], MEM_HEAD_DIM),
        'w_br_ssm': nrm(ks[23], (L, SSM_WIDTH, D_MODEL), SSM_WIDTH ** -0.5),
        'w_br_swa': nrm(ks[24], (L, SWA_Q_WIDTH, D_MODEL), SWA_Q_WIDTH ** -0.5),
        'w_br_mem': nrm(ks[25], (L, MEM_WIDTH, D_MODEL), MEM_WIDTH ** -0.5),
        'w_out': nrm(ks[26], (L, D_MODEL, D_MODEL), D_MODEL ** -0.5),
        'ffn_norm_g': gain(ks[27], D_MODEL),
        'w_router': nrm(ks[28], (L, D_MODEL, N_EXPERTS), D_MODEL ** -0.5),
        'b_router': nrm(ks[29], (L, N_EXPERTS), 0.01),
        'w_mlp1': nrm(ks[30], (L, N_EXPERTS, D_MODEL, 2 * D_EXPERT), D_MODEL ** -0.5),
        'b_mlp1': nrm(ks[31], (L, N_EXPERTS, 2 * D_EXPERT), 0.02),
        'w_mlp2': nrm(ks[32], (L, N_EXPERTS, D_EXPERT, D_MODEL), D_EXPERT ** -0.5),
        'b_mlp2': nrm(ks[33], (L, N_EXPERTS, D_MODEL), 0.02),
    }

def reference(x, mem, positions, attn_norm_g, mem_norm_g, w_in, b_gate,
              ssm_log_dt, ssm_a_re, ssm_a_im, ssm_b_re, ssm_b_im, ssm_c_re, ssm_c_im, ssm_d,
              w_glu_v, w_glu_g, swa_q_gain, swa_k_gain, swa_sinks,
              w_mem_kv, mem_q_gain, mem_k_gain,
              w_br_ssm, w_br_swa, w_br_mem, w_out,
              ffn_norm_g, w_router, b_router, w_mlp1, b_mlp1, w_mlp2, b_mlp2):
    bsz, seq, _ = x.shape
    offs = np.cumsum(IN_WIDTHS)[:-1].tolist()
    for l in range(DEPTH):
        h = rmsnorm(x, attn_norm_g[l], NORM_EPS)
        proj = h @ w_in[l]
        u, q_swa, k_swa, v_swa, q_mem, gate_logits = jnp.split(proj, offs, axis=-1)
        y_ssm = s5_branch(u, ssm_log_dt[l], ssm_a_re[l], ssm_a_im[l], ssm_b_re[l], ssm_b_im[l],
                          ssm_c_re[l], ssm_c_im[l], ssm_d[l], w_glu_v[l], w_glu_g[l])
        y_swa = swa_branch(q_swa.reshape(bsz, seq, SWA_Q_HEADS, HEAD_DIM),
                           k_swa.reshape(bsz, seq, SWA_KV_HEADS, HEAD_DIM),
                           v_swa.reshape(bsz, seq, SWA_KV_HEADS, HEAD_DIM),
                           positions, swa_q_gain[l], swa_k_gain[l], swa_sinks[l])
        mem_h = rmsnorm(mem, mem_norm_g[l], NORM_EPS)
        mk, mv = jnp.split(mem_h @ w_mem_kv[l], 2, axis=-1)
        y_mem = mem_branch(q_mem.reshape(bsz, seq, MEM_HEADS, MEM_HEAD_DIM),
                           mk.reshape(bsz, -1, MEM_HEADS, MEM_HEAD_DIM),
                           mv.reshape(bsz, -1, MEM_HEADS, MEM_HEAD_DIM),
                           mem_q_gain[l], mem_k_gain[l])
        gates = jax.nn.sigmoid((gate_logits + b_gate[l]).astype(jnp.float32)).astype(x.dtype)
        gates = gates.reshape(bsz, seq, N_BRANCH, D_MODEL)
        merged = (gates[:, :, 0] * (y_ssm @ w_br_ssm[l])
                  + gates[:, :, 1] * (y_swa @ w_br_swa[l])
                  + gates[:, :, 2] * (y_mem @ w_br_mem[l]))
        x = x + merged @ w_out[l]
        x = x + moe_ffn(rmsnorm(x, ffn_norm_g[l], NORM_EPS), w_router[l], b_router[l],
                        w_mlp1[l], b_mlp1[l], w_mlp2[l], b_mlp2[l])
    return x


_drawn_inputs = setup_inputs


def setup_inputs(seed=0):
    import zlib

    import numpy as np

    out = dict(_drawn_inputs(seed))
    spreads = {}
    factors = {'attn_norm_g': 2.759,
     'mem_norm_g': 8.0,
     'b_gate': 5.976,
     'ssm_a_re': 200.0,
     'swa_q_gain': 8.0,
     'swa_k_gain': 8.0,
     'swa_sinks': 183.453,
     'mem_q_gain': 8.0,
     'mem_k_gain': 6.871,
     'b_mlp1': 23.673,
     'b_mlp2': 27.093,
     'ssm_log_dt': 64.0,
     'ssm_a_im': 64.0,
     'ssm_b_re': 64.0,
     'ssm_b_im': 64.0,
     'ssm_c_re': 64.0,
     'ssm_c_im': 64.0,
     'ffn_norm_g': 5.947,
     'b_router': 7.408}
    for name, (base, spread) in spreads.items():
        noise = np.random.default_rng([zlib.crc32(name.encode()), seed]).standard_normal(out[name].shape)
        drawn = base * np.exp(spread * noise) if base else spread * noise
        out[name] = jnp.asarray(drawn.astype(out[name].dtype))
    for name, factor in factors.items():
        out[name] = (out[name] * factor).astype(out[name].dtype)
    return out
```

```python
from contextlib import ExitStack

import numpy as np
import concourse.bass as bass
import concourse.mybir as mybir
from concourse.alu_op_type import AluOpType as ALU

F32 = mybir.dt.float32
BF16 = mybir.dt.bfloat16
I32 = mybir.dt.int32
U32 = mybir.dt.uint32
ACT = mybir.ActivationFunctionType
AX = mybir.AxisListType

P = 128
D = 1024
SEQ = 256
TT = SEQ // P
KD = D // P
SSM = 512
GROUPS, GCH, STATE = 32, 16, 64
PAIRS = GROUPS // 2
CHUNK = 8
NCHUNK = SEQ // CHUNK
HEADS, KVH, HD = 16, 4, 64
ROPE_HALF = 8
ROPE_THETA = 500000.0
MH, MHD = 4, 128
EXPERTS, TOPK = 32, 4
SLOTS = 64
PASSES = SEQ // SLOTS
FF = 2048
NORM_EPS, QK_EPS = 1e-5, 1e-6
ALPHA, LIMIT = 1.702, 7.0
MAGIC = 1.5 * 2.0 ** 23
TWO_PI = (6.28125, 1.9340515136718750e-03, 1.2556659146e-06)
LN2 = (0.693359375, -2.12194440e-4)
PI_BOUND = 3.1415925
MASKED = -1e30

JOBS = (
    ["param", "cparam"]
    + [f"xT{t}{h}" for t in range(TT) for h in range(2)]
    + [f"u{t}" for t in range(TT)]
    + [f"q{n}{t}" for n in range(2) for t in range(TT)]
    + [f"kv{t}" for t in range(TT)]
    + [f"memT{t}{h}" for t in range(TT) for h in range(2)]
    + [f"mk{t}" for t in range(TT)] + [f"mv{t}" for t in range(TT)] + [f"qm{t}" for t in range(TT)]
    + ["lag0", "lag1"] + [f"in{n}" for n in range(8)] + ["uT0", "uT1", "xre", "xim"]
    + [f"qT{t}{h}" for t in range(TT) for h in range(2)] + [f"kT{t}" for t in range(TT)]
    + [f"qmT{t}" for t in range(TT)] + [f"mkT{t}" for t in range(TT)]
    + [f"y{h}{r}" for r in range(4) for h in range(2)]
)
for _h in range(MH):
    JOBS += [f"ms{_h}"]
GATE_JOBS = [f"gate{n}" for n in range(12)]
_steps = []
for _i in range(HEADS + 4):
    if _i < HEADS:
        _steps.append(f"s{_i}")
    if 2 <= _i < 2 + MH:
        _steps.append(f"mp{_i - 2}")
    if _i in (3, 5):
        _steps.append(f"mo{(_i - 3) // 2}")
    if 3 <= _i < 15:
        _steps.append(GATE_JOBS[_i - 3])
    if 3 <= _i < HEADS + 3:
        _steps.append(f"p{_i - 3}")
    if _i >= 7 and (_i - 7) % 4 == 0:
        _steps.append(f"pv{(_i - 7) // 4}")
JOBS += _steps
JOBS += ["gT0", "gT1", "gv0", "gv1", "gg0", "gg1"]
JOBS += [f"br{b}{i}" for b in (1, 0, 2) for i in range(4)]
JOBS += [f"o{t}{n}" for n in range(2) for t in range(TT)]
JOBS += [f"hT{t}{h}" for t in range(TT) for h in range(2)] + ["logit", "pos", "combT"]
BANK = {name: n % 8 for n, name in enumerate(JOBS)}
TURN = {name: n // 8 + 1 for n, name in enumerate(JOBS)}
TURNS = [len([n for n in range(len(JOBS)) if n % 8 == b]) for b in range(8)]

BLOCKS = (["u", "q0", "q1", "kv", "mk", "mv", "qm"] + [f"gate{n}" for n in range(6)]
          + ["glu", "swa0", "swa1", "ssm", "mem", "out0", "out1"])
RING = 4
SLOT_OF = {name: n % RING for n, name in enumerate(BLOCKS)}
LOADS_OF = {name: n // RING + 1 for n, name in enumerate(BLOCKS)}
LAST_JOB = {"u": "u1", "q0": "q01", "q1": "q11", "kv": "kv1", "mk": "mk1", "mv": "mv1", "qm": "qm1",
            "glu": "gg1", "swa0": "br11", "swa1": "br13", "ssm": "br03", "mem": "br23",
            "out0": "o10", "out1": "o11"} | {f"gate{n}": f"gate{2 * n + 1}" for n in range(6)}


def hybrid_layer(nc, x, mem, positions, attn_norm_g, mem_norm_g, w_in, b_gate,
                 ssm_log_dt, ssm_a_re, ssm_a_im, ssm_b_re, ssm_b_im, ssm_c_re, ssm_c_im, ssm_d,
                 w_glu_v, w_glu_g, swa_q_gain, swa_k_gain, swa_sinks,
                 w_mem_kv, mem_q_gain, mem_k_gain,
                 w_br_ssm, w_br_swa, w_br_mem, w_out,
                 ffn_norm_g, w_router, b_router, w_mlp1, b_mlp1, w_mlp2, b_mlp2, out):
    ctx = ExitStack()
    with ctx:
        def sb(name, shape, dt=F32):
            return ctx.enter_context(nc.sbuf_tensor(name, shape, dt))

        def sem(name):
            return ctx.enter_context(nc.semaphore(name))

        KB = 256
        ring = sb("ring", [P, RING, 4096])
        w2ring = sb("w2ring", [P, 32 * KB])
        arena = sb("arena", [P, 90 * KB])
        xres = sb("xres", [P, TT, D])

        def at(kb, *dims, base=None):
            size = int(np.prod(dims))
            off = int(kb * KB)
            v = (arena if base is None else base)[:, off:off + size]
            if len(dims) == 2:
                v = v.rearrange("p (a b) -> p a b", a=dims[0])
            if len(dims) == 3:
                v = v.rearrange("p (a b c) -> p a b c", a=dims[0], b=dims[1])
            if len(dims) == 4:
                v = v.rearrange("p (a b c d) -> p a b c d", a=dims[0], b=dims[1], c=dims[2])
            return v

        hT = at(0, KD, SEQ)
        h_tm = at(8, TT, D)
        q_tm = at(8, TT, D)
        mem_tm = at(16, TT, D)
        mk_tm = at(16, TT, 512)
        qm_tm = at(20, TT, 512)
        memT = at(24, KD, SEQ)
        mkT = at(24, MH, SEQ)
        qmT = at(28, MH, SEQ)
        mv_tm = at(32, TT, 512)
        kv_tm = at(36, TT, 512)
        kdup = at(40, TT, KVH, 2, HD)
        u_tm = at(44, TT, SSM)
        y_ssmT = at(44, 4, SEQ)
        y_memT = at(8, MH, SEQ)
        y_swaT = at(16, KD, SEQ)
        gates = at(48, 24, SEQ)
        ca_re = at(48, PAIRS, CHUNK + 1, GCH)
        ca_im = at(57, PAIRS, CHUNK + 1, GCH)
        u8 = at(66, CHUNK, SSM)
        u8g = at(24, 16, CHUNK, GCH)
        ab_tmp = at(66, PAIRS, CHUNK, GCH)
        b_re, b_im = at(74, PAIRS, GCH), at(75, PAIRS, GCH)
        bb_re, bb_im = at(76, PAIRS, GCH), at(77, PAIRS, GCH)
        c_re, c_im = at(78, PAIRS, GCH), at(79, PAIRS, GCH)
        c_raw = at(80, 2, 2, P)
        g_attn, g_mem = at(82, D), at(86, D)
        uT = at(82, GROUPS, NCHUNK)
        y_tm = at(82, TT, SSM)
        lag = at(86, 2, 4, P)
        st = at(86, 2, PAIRS, NCHUNK)
        gT = at(86, 4, SEQ)
        ab_re = at(0, PAIRS, CHUNK, GCH, base=w2ring)
        ab_im = at(8, PAIRS, CHUNK, GCH, base=w2ring)
        toep = at(0, 4, 2, 4, P, base=w2ring)
        win_re = at(16, PAIRS, P, base=w2ring)
        win_im = at(24, PAIRS, P, base=w2ring)
        ca_tmp = at(16, PAIRS, CHUNK + 1, GCH, base=w2ring)
        pT = at(0, 2, 4, 3, P, base=w2ring)
        mpT = at(12, 2, 2, SEQ, base=w2ring)
        qT = at(16, KD, SEQ, base=w2ring)
        kT = at(24, KVH, SEQ, base=w2ring)
        prob = at(72, 4, 3 * P)
        mprob = at(78, 2, TT, SEQ)
        merged = at(72, KD, SEQ)
        d_bc = at(28, SSM, base=w2ring)
        wr_sb = at(12, KD, EXPERTS)
        lg = at(13, TT, EXPERTS)
        comb = at(13.25, TT, EXPERTS)
        posm = at(13.5, TT, EXPERTS)
        ctmp = at(13.75, EXPERTS)
        top, topf, topw = at(14, TT, 8), at(14.25, TT, 8), at(14.5, TT, 8)
        h2 = at(0, TT, D)
        h2T = at(72, KD, SEQ)
        onehot = at(8, TT, 2 * SLOTS)
        onehot_w = at(9, 2, TT, 2 * SLOTS)
        bias_row = at(11, 2, SLOTS)
        hid_g, hid_l, hid_s = at(16, 2, 256), at(18, 2, 256), at(20, 2, 256)
        y_sb = at(22, 512)
        hgT = at(24, KD, 2 * SLOTS)
        actT = at(28, 4, P)
        scT = at(30, 2, SEQ)
        act_sb = at(32, 2, 2, 256)
        g_ffn = at(36, D)
        b2_sb = at(40, D)
        combT = at(44, SEQ)
        b1_sb = at(82, FF)

        ident = sb("ident", [P, P])
        ones_bf = sb("ones_bf", [P, P], BF16)
        before_bf = sb("before_bf", [P, P], BF16)
        mask = sb("mask", [P, 3 * P])
        iota2 = sb("iota2", [P, 2 * SLOTS])
        iota_e = sb("iota_e", [P, EXPERTS])
        prm = sb("prm", [74, P])
        ldt_raw = sb("ldt_raw", [48, 2])
        prmT = sb("prmT", [P, 74])
        tb = sb("tb", [P, 26, PAIRS])
        tbi = sb("tbi", [P, PAIRS], I32)
        pw_re = sb("pw_re", [P, CHUNK + 1, PAIRS])
        pw_im = sb("pw_im", [P, CHUNK + 1, PAIRS])
        a8 = sb("a8", [P, 2, 2, PAIRS])
        stp = sb("stp", [P, 2, 2, PAIRS])
        posi = sb("posi", [P, TT], I32)
        posf = sb("posf", [P, TT])
        rope = sb("rope", [P, 6, TT, ROPE_HALF])
        freq = sb("freq", [P, ROPE_HALF])
        gain_q = sb("gain_q", [P, HD])
        gain_k = sb("gain_k", [P, HD])
        sink = sb("sink", [P, HEADS])
        sq = sb("sq", [P, 512])
        rtmp = sq[:, :].rearrange("p (a b) -> p a b", a=4)
        ss = sb("ss", [P, 4])
        hs = sb("hs", [P, 10, 16])
        half = sb("half", [P, 16])
        smx = sb("smx", [P, 2, HEADS])
        snm = sb("snm", [P, 2, HEADS])
        sden = sb("sden", [P, 2, HEADS])
        ses = sb("ses", [P, 2, HEADS])
        msm = sb("msm", [P, 4, TT, MH])
        br_bc = sb("br_bc", [P, EXPERTS])
        topi = sb("topi", [P, TT, 8], U32)
        chosen = sb("chosen", [P, TT, EXPERTS], BF16)
        cmax = sb("cmax", [P, 1])
        count = sb("count", [P, 1], I32)

        ps = ctx.enter_context(nc.psum_tensor("ps", [P, 8, 512], F32))

        bank_full = [sem(f"bank_full{b}") for b in range(8)]
        bank_free = [sem(f"bank_free{b}") for b in range(8)]
        loaded = [sem(f"loaded{s}") for s in range(RING)]
        x_in, mem_in, gx_in, gm_in = sem("x_in"), sem("mem_in"), sem("gx_in"), sem("gm_in")
        prm_in, bc_in, cr_in, small_in, router_in = (
            sem("prm_in"), sem("bc_in"), sem("cr_in"), sem("small_in"), sem("router_in"))
        d_in, ldt_in, ldt_ready = sem("d_in"), sem("ldt_in"), sem("ldt_ready")
        late_in, gf_in = sem("late_in"), sem("gf_in")
        consts = sem("consts")
        sq_done = sem("sq_done")
        rstd_asked, rstd_done = sem("rstd_asked"), sem("rstd_done")
        pool_step = sem("pool_step")
        dve_step = sem("dve_step")
        act_step = sem("act_step")
        h_ready, mem_ready = sem("h_ready"), sem("mem_ready")
        angle_ready, sin_done = sem("angle_ready"), sem("sin_done")
        powers_ready, ab_ready, ca_ready = sem("powers_ready"), sem("ab_ready"), sem("ca_ready")
        toep_clear, toep_in = sem("toep_clear"), sem("toep_in")
        u8g_ready = sem("u8g_ready")
        u8_in, y8_out = sem("u8_in"), sem("y8_out")
        scan_done = sem("scan_done")
        qk_ready = sem("qk_ready")
        smax_ready, exp_done, prob_ready = sem("smax_ready"), sem("exp_done"), sem("prob_ready")
        mmax_ready, mexp_done, mprob_ready = sem("mmax_ready"), sem("mexp_done"), sem("mprob_ready")
        y_skip, gelu_done = sem("y_skip"), sem("gelu_done")
        merged_ready = sem("merged_ready")
        h2_ready, top_ready, topexp_done = sem("h2_ready"), sem("top_ready"), sem("topexp_done")
        chosen_ready, count_ready = sem("chosen_ready"), sem("count_ready")
        b1_clear = sem("b1_clear")
        acc_full = sem("acc_full")
        out_ready, out_done = sem("out_ready"), sem("out_done")
        w1_loaded = [sem(f"w1_loaded{k}") for k in range(KD)]
        w2_loaded = [sem(f"w2_loaded{k}") for k in range(KD)]
        w1_used, w2_used = sem("w1_used"), sem("w2_used")
        hid_free = sem("hid_free")
        glu_in, sig_done, act_ready = sem("glu_in"), sem("sig_done"), sem("act_ready")
        actT_full, actT_ready = sem("actT_full"), sem("actT_ready")
        y_ready = sem("y_ready")
        scattered = sem("scattered")
        gather_full, gather_ready = sem("gather_full"), sem("gather_ready")
        scT_full, scT_ready = sem("scT_full"), sem("scT_ready")
        onehot_ready, weighted_ready, row_ready = (
            sem("onehot_ready"), sem("weighted_ready"), sem("row_ready"))
        moe_dve, pass_step = sem("moe_dve"), sem("pass_step")

        block = ctx.enter_context(nc.Block())

        def bank(name):
            return ps[:, BANK[name], :]

        def wait_full(eng, name):
            eng.wait_ge(bank_full[BANK[name]], TURN[name])

        def wait_emptied(eng, name):
            eng.wait_ge(bank_free[BANK[name]], TURN[name])

        acc = [[ps[:, 2 * t + n, :] for n in range(2)] for t in range(TT)]
        H0, YB, TB = 4, 6, 7

        @block.sync
        def _(sp):
            win = w_in.rearrange("(k p) n -> p k n", p=P)
            wkv = w_mem_kv.rearrange("(k p) n -> p k n", p=P)
            wsw = w_br_swa.rearrange("(k p) n -> p k n", p=P)
            wo = w_out.rearrange("(k p) n -> p k n", p=P)

            def load_block(n):
                name = BLOCKS[n]
                if n >= RING:
                    wait_full(sp, LAST_JOB[BLOCKS[n - RING]])
                slot = ring[:, n % RING, :]
                slot8 = slot.rearrange("p (k n) -> p k n", k=KD)
                if name == "glu":
                    for i, w in enumerate((w_glu_v, w_glu_g)):
                        sp.dma_start(slot[:, i * 2048:(i + 1) * 2048].rearrange("p (k n) -> p k n", k=4),
                                     w.rearrange("(k p) n -> p k n", p=P)).then_inc(loaded[n % RING], 8 * 2)
                    return
                if name in ("ssm", "mem"):
                    src = (w_br_ssm if name == "ssm" else w_br_mem).rearrange("(k p) n -> p k n", p=P)
                    sp.dma_start(slot.rearrange("p (k n) -> p k n", k=4), src).then_inc(loaded[n % RING], 16)
                    return
                col = {"u": 0, "q0": 512, "q1": 1024, "kv": 1536, "qm": 2048}
                if name in col:
                    src = win[:, :, col[name]:col[name] + 512]
                elif name.startswith("gate"):
                    src = win[:, :, 2560 + 512 * int(name[4:]):3072 + 512 * int(name[4:])]
                elif name in ("mk", "mv"):
                    src = wkv[:, :, 0:512] if name == "mk" else wkv[:, :, 512:1024]
                else:
                    n0 = 512 * int(name[-1])
                    src = (wsw if name.startswith("swa") else wo)[:, :, n0:n0 + 512]
                sp.dma_start(slot8, src).then_inc(loaded[n % RING], 16)

            sp.dma_start(xres[:, :, :], x.rearrange("(t p) n -> p t n", p=P)).then_inc(x_in, 16)
            sp.dma_start(g_attn, attn_norm_g.unsqueeze(0).broadcast_to([P, D])).then_inc(gx_in, 16)
            for n in range(11):
                if n == 2:
                    sp.dma_start(mem_tm, mem.rearrange("(t p) n -> p t n", p=P)).then_inc(mem_in, 16)
                    sp.dma_start(g_mem, mem_norm_g.unsqueeze(0).broadcast_to([P, D])).then_inc(gm_in, 16)
                load_block(n)
            wait_emptied(sp, "u0")
            wait_emptied(sp, "u1")
            sp.wait_ge(ab_ready, 1)
            wait_full(sp, "lag1")
            for t in range(TT):
                sp.dma_start(u8[16 * t:16 * t + 16, :, :], u_tm[:, t, :]).then_inc(u8_in, 16)
            sp.wait_ge(toep_clear, 1)
            wait_emptied(sp, "lag0")
            wait_emptied(sp, "lag1")
            for t in range(CHUNK):
                w = P - GCH * t
                for j in range(4):
                    sp.dma_start(toep[GCH * t:GCH * t + GCH, j, :, :, GCH * t:P],
                                 lag[32 * j:32 * j + GCH, :, :, 0:w]).then_inc(toep_in, 16)
            for r in range(4):
                for h in range(2):
                    wait_emptied(sp, f"y{h}{r}")
            for t in range(TT):
                sp.dma_start(y_tm[:, t, :], u8[16 * t:16 * t + 16, :, :]).then_inc(y8_out, 16)
            wait_full(sp, "xim")
            sp.dma_start(d_bc, ssm_d.unsqueeze(0).broadcast_to([P, SSM])).then_inc(d_in, 16)
            wait_full(sp, "qT11")
            sp.dma_start(wr_sb, w_router.rearrange("(k p) n -> p k n", p=P)).then_inc(router_in, 16)
            for n in range(11, len(BLOCKS)):
                load_block(n)

            def load_experts(p):
                w1v = w_mlp1.rearrange("e (k p) n -> e k p n", p=P)
                w2v = w_mlp2.rearrange("e (k p) n -> e k p n", p=P)

                def first_matrix(e, first):
                    for k in range(KD):
                        if first:
                            wait_full(sp, LAST_JOB[BLOCKS[len(BLOCKS) - RING + k // 2]])
                        else:
                            sp.wait_ge(w1_used, (e + EXPERTS * p) * KD + (k + 1 - KD))
                        sp.dma_start(ring[:, k // 2, (k % 2) * 2048:(k % 2) * 2048 + 2048],
                                     w1v[e, k]).then_inc(w1_loaded[k], 16)

                def second_matrix(e, first):
                    for k in range(KD):
                        if not first:
                            sp.wait_ge(w2_used, (e + EXPERTS * p) * KD + (k + 1 - KD))
                        sp.dma_start(w2ring[:, k * D:(k + 1) * D], w2v[e, k]).then_inc(w2_loaded[k], 16)

                return first_matrix, second_matrix

            first_matrix, second_matrix = load_experts(0)
            wait_full(sp, "gg1")
            sp.wait_ge(b1_clear, 1)
            sp.dma_start(b1_sb[0:EXPERTS, :], b_mlp1).then_inc(late_in, 16)
            wait_full(sp, "kT1")
            sp.dma_start(b2_sb[0:EXPERTS, :], b_mlp2).then_inc(late_in, 16)
            wait_full(sp, "pv3")
            sp.dma_start(g_ffn, ffn_norm_g.unsqueeze(0).broadcast_to([P, D])).then_inc(gf_in, 16)
            wait_full(sp, "mo1")
            second_matrix(0, True)
            first_matrix(0, True)
            first_matrix(1, False)
            with sp.Fori(1, EXPERTS - 1) as e:
                first_matrix(e + 1, False)
                second_matrix(e, False)
            second_matrix(EXPERTS - 1, False)
            sp.wait_ge(count_ready, 1)
            most = sp.value_load(count[0:1, 0:1], min_val=0, max_val=SEQ)
            with sp.Fori(1, PASSES) as p:
                with sp.If(most > p * SLOTS):
                    first_matrix, second_matrix = load_experts(p)
                    first_matrix(0, False)
                    with sp.Fori(0, EXPERTS - 1) as e:
                        first_matrix(e + 1, False)
                        second_matrix(e, False)
                    second_matrix(EXPERTS - 1, False)
            sp.wait_ge(out_ready, TT)
            sp.dma_start(out.rearrange("(t p) n -> p t n", p=P), xres[:, :, :]).then_inc(out_done, 16)
            sp.wait_ge(out_done, 16)

        @block.gpsimd
        def _(pool):
            steps = [0]

            def link(ins):
                steps[0] += 1
                ins.then_inc(pool_step, 1)
                pool.wait_ge(pool_step, steps[0])

            link(pool.memset(half[:, :], -0.5))
            link(pool.memset(ident[:, :], 0.0))
            pool.affine_select(out=ident[:, :], in_=ident[:, :], compare_op=ALU.not_equal, fill=1.0,
                               base=0, pattern=[[-1, P]], channel_multiplier=1).then_inc(consts, 1)
            link(pool.memset(mask[:, :], 0.0))
            link(pool.affine_select(out=mask[:, 0:P], in_=mask[:, 0:P], compare_op=ALU.is_ge, fill=MASKED,
                                    base=0, pattern=[[-1, P]], channel_multiplier=1))
            link(pool.affine_select(out=mask[:, P:2 * P], in_=mask[:, P:2 * P], compare_op=ALU.is_gt,
                                    fill=MASKED, base=0, pattern=[[1, P]], channel_multiplier=-1))
            pool.affine_select(out=mask[:, 2 * P:3 * P], in_=mask[:, 2 * P:3 * P], compare_op=ALU.is_ge,
                               fill=MASKED, base=0, pattern=[[-1, P]],
                               channel_multiplier=1).then_inc(consts, 1)
            link(pool.memset(ones_bf[:, :], 1.0))
            link(pool.memset(before_bf[:, :], 1.0))
            pool.affine_select(out=before_bf[:, :], in_=before_bf[:, :], compare_op=ALU.is_gt, fill=0.0,
                               base=0, pattern=[[1, P]], channel_multiplier=-1).then_inc(consts, 1)
            pool.iota(iota2[:, :], pattern=[[0, 2], [1, SLOTS]], base=0, channel_multiplier=0,
                      allow_small_or_imprecise_dtypes=True).then_inc(consts, 1)
            pool.iota(iota_e[:, :], pattern=[[1, EXPERTS]], base=0, channel_multiplier=0,
                      allow_small_or_imprecise_dtypes=True).then_inc(consts, 1)
            for i in range(ROPE_HALF):
                f = float(np.float32(ROPE_THETA ** (-i / ROPE_HALF)))
                last = pool.memset(freq[:, i:i + 1], f)
            last.then_inc(consts, 1)

            def rstd(v, n, width, eps):
                link(pool.tensor_scalar(v, v, 1.0 / width, eps, ALU.mult, ALU.add))
                pool.tensor_tensor(v, v, half[:, 0:n], ALU.pow).then_inc(rstd_done, 1)

            for i in range(2):
                pool.wait_ge(sq_done, 2 * i + 2)
                rstd(ss[:, 2 * i:2 * i + 2], 2, D, NORM_EPS)
            pool.wait_ge(powers_ready, 1)

            def over_t(v):
                return v.unsqueeze(2).broadcast_to([P, PAIRS, CHUNK, GCH])

            def over_c(v):
                return v[:, CHUNK - 1::-1, :].rearrange("p t q -> p q t").unsqueeze(3)\
                    .broadcast_to([P, PAIRS, CHUNK, GCH])

            def table(dst, b0, p0, b1, p1, op):
                link(pool.tensor_tensor(dst, over_t(b0), over_c(p0), ALU.mult))
                link(pool.tensor_tensor(ab_tmp, over_t(b1), over_c(p1), ALU.mult))
                return pool.tensor_tensor(dst, dst, ab_tmp, op)

            link(table(ab_re, bb_re, pw_re, bb_im, pw_im, ALU.subtract))
            table(ab_im, bb_re, pw_im, bb_im, pw_re, ALU.add).then_inc(ab_ready, 1)
            widths = [HD] * 6 + [MHD] * 4
            counts = [8] * 4 + [4] * 6
            for i in range(6):
                pool.wait_ge(rstd_asked, i + 1)
                rstd(hs[:, i, 0:counts[i]], counts[i], widths[i], QK_EPS)
            wait_full(pool, "in7")
            wait_full(pool, "lag1")
            pool.memset(at(0, 4096, base=w2ring), 0.0).then_inc(toep_clear, 1)
            for i in range(6, 10):
                pool.wait_ge(rstd_asked, i + 1)
                rstd(hs[:, i, 0:counts[i]], counts[i], widths[i], QK_EPS)
            wait_full(pool, "gg1")
            pool.memset(b1_sb, 0.0).then_inc(b1_clear, 1)
            pool.wait_ge(h2_ready, 1)
            pool.wait_ge(sq_done, 6)
            rstd(ss[:, 0:2], 2, D, NORM_EPS)

        @block.scalar
        def _(act):
            def row(v):
                return v.unsqueeze(0)

            for i, v in enumerate((ssm_a_re, ssm_a_im)):
                act.dma_start(prm[16 * i:16 * i + 16, :], v.rearrange("(q h) s -> q (h s)", h=2)).then_inc(prm_in, 16)
            act.dma_start(ldt_raw[32:48, :], ssm_log_dt.rearrange("(q h) -> q h", h=2)).then_inc(ldt_in, 16)
            act.dma_start(prm[48:72, :], b_gate.rearrange("(c p) -> c p", p=P)).then_inc(prm_in, 16)
            act.dma_start(prm[72:73, :], row(mem_q_gain)).then_inc(prm_in, 16)
            act.dma_start(prm[73:74, :], row(mem_k_gain)).then_inc(prm_in, 16)
            for i, v in enumerate((ssm_c_re, ssm_c_im)):
                for r in range(2):
                    src = v.rearrange("(r q h) c s -> r h q c s", r=2, h=2)[r]
                    for h in range(2):
                        act.dma_start(c_raw[:, i, r, STATE * h:STATE * h + STATE], src[h]).then_inc(cr_in, 16)
            for v, dst in ((ssm_b_re, b_re), (ssm_b_im, b_im)):
                for h in range(2):
                    act.dma_start(dst[STATE * h:STATE * h + STATE, :, :],
                                  v.rearrange("(q h) s c -> h s q c", h=2)[h]).then_inc(bc_in, 16)
            for t in range(TT):
                act.dma_start(posi[:, t:t + 1], positions[P * t:P * t + P].unsqueeze(1)).then_inc(small_in, 16)
            act.dma_start(gain_q[:, :], row(swa_q_gain).broadcast_to([P, HD])).then_inc(small_in, 16)
            act.dma_start(gain_k[:, :], row(swa_k_gain).broadcast_to([P, HD])).then_inc(small_in, 16)
            act.dma_start(sink[:, :], row(swa_sinks).broadcast_to([P, HEADS])).then_inc(small_in, 16)
            act.dma_start(br_bc[:, :], row(b_router).broadcast_to([P, EXPERTS])).then_inc(router_in, 16)

            def empty(name, dst, src):
                wait_full(act, name)
                nc.scalar.copy(dst, src).then_inc(bank_free[BANK[name]], 1)

            def square(v, n):
                nc.scalar.activation(at(24, D), v, ACT.Square,
                                     accum_out=ss[:, n:n + 1]).then_inc(sq_done, 1)

            act.wait_ge(x_in, 16)
            square(xres[:, 0, :], 0)
            act.wait_ge(sq_done, 1)
            square(xres[:, 1, :], 1)
            act.wait_ge(mem_in, 16)
            for t in range(TT):
                act.wait_ge(sq_done, 2 + t)
                square(mem_tm[:, t, :], 2 + t)

            wait_full(act, "param")
            nc.scalar.copy(prmT[:, :], bank("param")[:, 0:74]).then_inc(bank_free[BANK["param"]], 1)
            wait_full(act, "cparam")
            cp = bank("cparam").rearrange("p (i r n) -> p i (r n)", i=2, r=2)
            nc.scalar.copy(at(78, 2, 256), cp).then_inc(bank_free[BANK["cparam"]], 1)
            for t in range(TT):
                for h in range(2):
                    empty(f"xT{t}{h}", hT[:, 4 * h:4 * h + 4, P * t:P * t + P],
                          bank(f"xT{t}{h}").rearrange("p (k n) -> p k n", k=4))
            for t in range(TT):
                empty(f"u{t}", u_tm[:, t, :], bank(f"u{t}"))
            act.wait_ge(angle_ready, 1)
            nc.scalar.activation(tb[:, 10:12, :], tb[:, 8:10, :], ACT.Sin).then_inc(sin_done, 1)
            for n in range(2):
                for t in range(TT):
                    empty(f"q{n}{t}", q_tm[:, t, 512 * n:512 * n + 512], bank(f"q{n}{t}"))
            for t in range(TT):
                empty(f"kv{t}", kv_tm[:, t, :], bank(f"kv{t}"))
            for t in range(TT):
                for h in range(2):
                    empty(f"memT{t}{h}", memT[:, 4 * h:4 * h + 4, P * t:P * t + P],
                          bank(f"memT{t}{h}").rearrange("p (k n) -> p k n", k=4))
            for t in range(TT):
                empty(f"mk{t}", mk_tm[:, t, :], bank(f"mk{t}"))
            for t in range(TT):
                empty(f"mv{t}", mv_tm[:, t, :], bank(f"mv{t}"))
            for t in range(TT):
                empty(f"qm{t}", qm_tm[:, t, :], bank(f"qm{t}"))
            act.wait_ge(angle_ready, 2)
            nc.scalar.activation(rope[:, 2:4, :, :], rope[:, 0:2, :, :], ACT.Sin).then_inc(sin_done, 1)
            for h in range(2):
                empty(f"lag{h}", lag[:, h, :, :].rearrange("p s n -> p (s n)"), bank(f"lag{h}"))
            for n in range(8):
                wait_full(act, f"in{n}")
                v = bank(f"in{n}").rearrange("p (q i n) -> p q i n", q=2, i=2)
                nc.scalar.copy(win_re[:, 2 * n:2 * n + 2, :], v[:, :, 0, :]).then_inc(act_step, 1)
                nc.scalar.copy(win_im[:, 2 * n:2 * n + 2, :], v[:, :, 1, :]).then_inc(bank_free[BANK[f"in{n}"]], 1)
            act.wait_ge(u8_in, 32)
            for n in range(2):
                nc.scalar.copy(u8g[0:NCHUNK, :, :, :].rearrange("p g t c -> p t g c"),
                               u8[0:NCHUNK, :, 256 * n:256 * n + 256].rearrange("p t (g c) -> p t g c", c=GCH))\
                    .then_inc(u8g_ready, 1)
                empty(f"uT{n}", uT[:, 16 * n:16 * n + 16, :].rearrange("p g n -> p (g n)"), bank(f"uT{n}"))
            for t in range(TT):
                for h in range(2):
                    empty(f"qT{t}{h}", qT[:, 4 * h:4 * h + 4, P * t:P * t + P],
                          bank(f"qT{t}{h}").rearrange("p (k n) -> p k n", k=4))
            for t in range(TT):
                empty(f"kT{t}", kT[:, :, P * t:P * t + P], bank(f"kT{t}").rearrange("p (k n) -> p k n", k=4))
            for name, dst, col in (("qmT", qmT, 72), ("mkT", mkT, 73)):
                for t in range(TT):
                    wait_full(act, f"{name}{t}")
                    nc.scalar.mul(dst[:, :, P * t:P * t + P],
                                  bank(f"{name}{t}").rearrange("p (k n) -> p k n", k=4),
                                  prmT[:, col:col + 1]).then_inc(bank_free[BANK[f"{name}{t}"]], 1)
            for r in range(4):
                for h in range(2):
                    wait_full(act, f"y{h}{r}")
                    src = bank(f"y{h}{r}")[0:NCHUNK, :].rearrange("p (q t c) -> p t q c", q=4, t=CHUNK)
                    dst = u8[0:NCHUNK, :, :].rearrange("p t (q h c) -> p t q h c", h=2, c=GCH)
                    for q in range(4):
                        ins = nc.scalar.copy(dst[:, :, 4 * r + q, h, :], src[:, :, q, :])
                    ins.then_inc(bank_free[BANK[f"y{h}{r}"]], 1)

            def mem_exp(h):
                act.wait_ge(mmax_ready, h + 1)
                if h >= 2:
                    wait_full(act, f"mp{h - 2}")
                v = bank(f"ms{h}").rearrange("p (t n) -> p t n", t=TT)
                nc.scalar.activation(mprob[:, h % 2, 0, :], v[:, 0, :], ACT.Exp, bias=msm[:, 1, 0, h:h + 1],
                                     scale=MHD ** -0.5, accum_out=msm[:, 2, 0, h:h + 1]).then_inc(act_step, 1)
                nc.scalar.activation(mprob[:, h % 2, 1, :], v[:, 1, :], ACT.Exp, bias=msm[:, 1, 1, h:h + 1],
                                     scale=MHD ** -0.5, accum_out=msm[:, 2, 1, h:h + 1])\
                    .then_inc(bank_free[BANK[f"ms{h}"]], 1)

            def swa_exp(h):
                act.wait_ge(smax_ready, h + 1)
                s = prob[:, h % 4, :]
                for b, (lo, hi) in enumerate(((0, P), (P, 3 * P))):
                    nc.scalar.activation(s[:, lo:hi], s[:, lo:hi], ACT.Exp, bias=snm[:, b, h:h + 1],
                                         accum_out=sden[:, b, h:h + 1]).then_inc(exp_done, 1)
                nc.scalar.activation(ses[:, :, h:h + 1], snm[:, :, h:h + 1], ACT.Exp,
                                     bias=sink[:, h:h + 1]).then_inc(exp_done, 1)

            act.wait_ge(small_in, 80)
            act.wait_ge(y8_out, 32)
            mem_exp(0)
            mem_exp(1)
            for name in _steps:
                if name.startswith("mp"):
                    h = int(name[2:])
                    if h >= 2:
                        wait_full(act, f"mo{h // 2 - 1}")
                    empty(name, mpT[:, h % 2, :, :].rearrange("p a b -> p (a b)"), bank(name))
                    if h + 2 < MH:
                        mem_exp(h + 2)
                elif name.startswith("mo"):
                    h = int(name[2:])
                    empty(name, y_memT[:, 2 * h:2 * h + 2, :].rearrange("p a b -> p (a b)"), bank(name))
                elif name.startswith("gate"):
                    n = int(name[4:])
                    wait_full(act, name)
                    for c in range(2):
                        ins = nc.scalar.activation(gates[:, 2 * n + c, :], bank(name)[:, SEQ * c:SEQ * c + SEQ],
                                                   ACT.Sigmoid, bias=prmT[:, 48 + 2 * n + c:49 + 2 * n + c])
                    ins.then_inc(bank_free[BANK[name]], 1)
                elif name.startswith("pv"):
                    j = int(name[2:])
                    empty(name, y_swaT[:, 2 * j:2 * j + 2, :].rearrange("p a b -> p (a b)"), bank(name))
                elif name.startswith("p"):
                    h = int(name[1:])
                    if h >= 8 and h % 4 == 0:
                        wait_full(act, f"pv{h // 4 - 2}")
                    empty(name, pT[:, h // 4 % 2, h % 4, :, :].rearrange("p a b -> p (a b)"),
                          bank(name)[:, 0:3 * P])
                elif name.startswith("s"):
                    swa_exp(int(name[1:]))
            act.wait_ge(y_skip, 1)
            nc.scalar.activation(y_tm, y_tm, ACT.Gelu_apprx_tanh).then_inc(gelu_done, 1)
            for t in range(TT):
                empty(f"gT{t}", gT[:, :, P * t:P * t + P], bank(f"gT{t}").rearrange("p (k n) -> p k n", k=4))
            for n in range(2):
                wait_full(act, f"gg{n}")
                nc.scalar.activation(sq[:, :], bank(f"gg{n}"), ACT.Sigmoid).then_inc(bank_free[BANK[f"gg{n}"]], 1)
                wait_emptied(act, f"gv{n}")
            for t in range(TT):
                act.wait_ge(h2_ready, 1)
                act.wait_ge(sq_done, 4 + t)
                nc.scalar.activation(at(52, D), xres[:, t, :], ACT.Square,
                                     accum_out=ss[:, t:t + 1]).then_inc(sq_done, 1)
            for t in range(TT):
                for h in range(2):
                    empty(f"hT{t}{h}", h2T[:, 4 * h:4 * h + 4, P * t:P * t + P],
                          bank(f"hT{t}{h}").rearrange("p (k n) -> p k n", k=4))
            act.wait_ge(top_ready, 1)
            for t in range(TT):
                ins = nc.scalar.activation(topw[:, t, 0:TOPK], top[:, t, 0:TOPK], ACT.Exp, bias=topw[:, t, 4:5],
                                           accum_out=topw[:, t, 5:6])
                ins.then_inc(topexp_done, 1)
            wait_full(act, "combT")
            nc.scalar.copy(combT[0:EXPERTS, :], bank("combT")[0:EXPERTS, 0:SEQ]).then_inc(bank_free[BANK["combT"]], 1)

            def gather_half(i, n):
                act.wait_ge(gather_full, 2 * i + (n + 1))
                nc.scalar.copy(hgT[:, 4 * n:4 * n + 4, :].rearrange("p k n -> p (k n)"),
                               ps[:, TB, :]).then_inc(gather_ready, 1)

            def act_transposed(e, c):
                act.wait_ge(actT_full, e + (c + 1))
                nc.scalar.copy(actT.rearrange("p a b -> p (a b)"), ps[:, TB, :]).then_inc(actT_ready, 1)

            def sigmoid(e, c):
                act.wait_ge(glu_in, e + (c + 1))
                nc.scalar.activation(hid_s, hid_g, ACT.Sigmoid, scale=ALPHA).then_inc(sig_done, 1)

            def empty_y(e, c):
                act.wait_ge(w2_used, (e + (c + 1)) * KD)
                nc.scalar.copy(y_sb, ps[:, YB, :]).then_inc(y_ready, 1)

            def moe(p):
                gather_half(p * 16, 0)
                gather_half(p * 16, 1)

                def pair(i, first=False, last=False):
                    e = 2 * i
                    if not first:
                        act_transposed(e, -1)
                    sigmoid(e, 0)
                    if not first:
                        empty_y(e, -1)
                    act.wait_ge(scT_full, i + 1)
                    nc.scalar.copy(scT.rearrange("p a b -> p (a b)"), ps[:, TB, :]).then_inc(scT_ready, 1)
                    if not last:
                        gather_half(i + 1, 0)
                    act_transposed(e, 0)
                    sigmoid(e, 1)
                    if not last:
                        gather_half(i + 1, 1)
                    empty_y(e, 0)

                pair(p * 16, first=True)
                with act.Fori(1, 15) as i:
                    pair(i + p * 16)
                pair(p * 16 + 15, last=True)
                act_transposed(p * EXPERTS, EXPERTS - 1)
                empty_y(p * EXPERTS, EXPERTS - 1)

            moe(0)
            act.wait_ge(count_ready, 1)
            most = act.value_load(count[0:1, 0:1], min_val=0, max_val=SEQ)
            with act.Fori(1, PASSES) as p:
                with act.If(most > p * SLOTS):
                    moe(p)

        @block.tensor
        def _(pe):
            mm = nc.tensor.matmul

            def begin(name):
                if TURN[name] > 1:
                    pe.wait_ge(bank_free[BANK[name]], TURN[name] - 1)
                return bank(name)

            def end(ins, name):
                ins.then_inc(bank_full[BANK[name]], 1)

            def transposes(name, tiles):
                o, col = begin(name), 0
                for t in tiles:
                    n = t.shape[0]
                    ins = nc.tensor.transpose(o[0:t.free_size(), col:col + n], t, ident[0:n, 0:n])
                    col += n
                end(ins, name)

            def wait_block(name):
                pe.wait_ge(loaded[SLOT_OF[name]], 16 * LOADS_OF[name] + (16 if name == "glu" else 0)
                           + (16 if SLOT_OF[name] == SLOT_OF["glu"] and BLOCKS.index(name) > BLOCKS.index("glu") else 0))
                return ring[:, SLOT_OF[name], :]

            def token_major(name, blk, lhs, t):
                w = wait_block(blk).rearrange("p (k n) -> p k n", k=KD)
                o = begin(name)
                for k in range(KD):
                    ins = mm(o, lhs[:, k, P * t:P * t + P], w[:, k, :], start=(k == 0), stop=(k == KD - 1))
                end(ins, name)

            pe.wait_ge(consts, 1)
            pe.wait_ge(prm_in, 5 * 16)
            pe.wait_ge(ldt_ready, 1)
            transposes("param", [prm[:, :]])
            pe.wait_ge(cr_in, 8 * 16)
            transposes("cparam", [c_raw[:, i, r, :] for i in range(2) for r in range(2)])
            for t in range(TT):
                pe.wait_ge(h_ready, t + 1)
                for h in range(2):
                    transposes(f"xT{t}{h}", [h_tm[:, t, P * k:P * k + P] for k in range(4 * h, 4 * h + 4)])
            for t in range(TT):
                for h in range(2):
                    wait_emptied(pe, f"xT{t}{h}")
            for t in range(TT):
                token_major(f"u{t}", "u", hT, t)
            for n in range(2):
                for t in range(TT):
                    token_major(f"q{n}{t}", f"q{n}", hT, t)
            for t in range(TT):
                token_major(f"kv{t}", "kv", hT, t)
            for t in range(TT):
                pe.wait_ge(mem_ready, t + 1)
                for h in range(2):
                    transposes(f"memT{t}{h}", [mem_tm[:, t, P * k:P * k + P] for k in range(4 * h, 4 * h + 4)])
            for t in range(TT):
                for h in range(2):
                    wait_emptied(pe, f"memT{t}{h}")
            for t in range(TT):
                token_major(f"mk{t}", "mk", memT, t)
            for t in range(TT):
                token_major(f"mv{t}", "mv", memT, t)
            for t in range(TT):
                token_major(f"qm{t}", "qm", hT, t)

            pe.wait_ge(ab_ready, 1)
            pe.wait_ge(ca_ready, 1)
            for h in range(2):
                o = begin(f"lag{h}")
                s = slice(STATE * h, STATE * h + STATE)
                for q in range(PAIRS):
                    dst = o[32 * (q % 4):32 * (q % 4) + GCH, P * (q // 4):P * (q // 4) + P]
                    mm(dst, ab_re[s, q, CHUNK - 1, :], ca_re[s, q, 0:CHUNK, :], start=True, stop=False,
                       skip_group_check=True)
                    ins = mm(dst, ab_im[s, q, CHUNK - 1, :], ca_im[s, q, 0:CHUNK, :], start=False, stop=True,
                             skip_group_check=True)
                end(ins, f"lag{h}")
            for n in range(8):
                transposes(f"in{n}", [v[:, 2 * n + q, :, :].rearrange("p t c -> p (t c)")
                                      for q in range(2) for v in (ab_re, ab_im)])
            for n in range(2):
                pe.wait_ge(u8g_ready, n + 1)
                transposes(f"uT{n}", [u8g[0:NCHUNK, g, :, :].rearrange("p t c -> p (t c)") for g in range(16)])
            for n in range(8):
                wait_emptied(pe, f"in{n}")
            for n in range(2):
                wait_emptied(pe, f"uT{n}")
            for name, w in (("xre", win_re), ("xim", win_im)):
                o = begin(name)
                for q in range(PAIRS):
                    for h in range(2):
                        ins = mm(o[STATE * h:STATE * h + STATE, NCHUNK * q:NCHUNK * q + NCHUNK],
                                 w[:, q, STATE * h:STATE * h + STATE], uT[:, 2 * q + h, :],
                                 start=True, stop=True, skip_group_check=True)
                end(ins, name)
            pe.wait_ge(qk_ready, 4)
            for t in range(TT):
                for h in range(2):
                    transposes(f"qT{t}{h}", [q_tm[:, t, P * k:P * k + P] for k in range(4 * h, 4 * h + 4)])
            pe.wait_ge(qk_ready, 6)
            for t in range(TT):
                transposes(f"kT{t}", [kdup[:, t, j, :, :].rearrange("p a b -> p (a b)") for j in range(KVH)])
            pe.wait_ge(qk_ready, 8)
            for t in range(TT):
                transposes(f"qmT{t}", [qm_tm[:, t, P * h:P * h + P] for h in range(MH)])
            pe.wait_ge(qk_ready, 10)
            for t in range(TT):
                transposes(f"mkT{t}", [mk_tm[:, t, P * h:P * h + P] for h in range(MH)])
            pe.wait_ge(scan_done, 1)
            pe.wait_ge(toep_in, 32 * 16)
            for r in range(4):
                for h in range(2):
                    o = begin(f"y{h}{r}")
                    s = slice(STATE * h, STATE * h + STATE)
                    for i in range(4):
                        ins = mm(o[0:NCHUNK, P * i:P * i + P], uT[:, 2 * (4 * r + i) + h, :],
                                 toep[:, i, h, r, :], start=(i == 0), stop=False, skip_group_check=True)
                    for i in range(4):
                        q = 4 * r + i
                        mm(o[0:NCHUNK, P * i:P * i + P], st[s, 0, q, :], ca_re[s, q, 1:CHUNK + 1, :],
                           start=False, stop=False, skip_group_check=True)
                        ins = mm(o[0:NCHUNK, P * i:P * i + P], st[s, 1, q, :], ca_im[s, q, 1:CHUNK + 1, :],
                                 start=False, stop=(i == 3), skip_group_check=True)
                    end(ins, f"y{h}{r}")

            for h in range(MH):
                for n in ("qmT", "mkT"):
                    for t in range(TT):
                        wait_emptied(pe, f"{n}{t}")
                o = begin(f"ms{h}")
                for t in range(TT):
                    ins = mm(o[:, SEQ * t:SEQ * t + SEQ], qmT[:, h, P * t:P * t + P], mkT[:, h, :],
                             start=True, stop=True, skip_group_check=True)
                end(ins, f"ms{h}")

            def scores(h):
                o = begin(f"s{h}")
                s = slice(HD * (h % 2), HD * (h % 2) + HD)
                mm(o[:, 0:P], qT[s, h // 2, 0:P], kT[s, h // 4, 0:P], start=True, stop=True, skip_group_check=True)
                end(mm(o[:, P:3 * P], qT[s, h // 2, P:SEQ], kT[s, h // 4, :], start=True, stop=True,
                       skip_group_check=True), f"s{h}")

            def weighted_values(j):
                o = begin(f"pv{j}").rearrange("p (a n) -> p a n", a=2)
                for qb, blk, kb, st_, sp_ in ((0, 0, 0, True, True), (1, 1, 0, True, False), (1, 2, 1, False, True)):
                    for par in range(2):
                        ins = mm(o[HD * par:HD * par + HD, :, P * qb:P * qb + P],
                                 kv_tm[:, kb, 256 + HD * j:256 + HD * j + HD], pT[:, j % 2, par::2, blk, :],
                                 start=st_, stop=sp_, skip_group_check=True)
                end(ins, f"pv{j}")

            def channel_major(name, w, rhs, chans, kn):
                o = begin(name)
                for c, ch in enumerate(chans):
                    for k in range(kn):
                        ins = mm(o[:, SEQ * c:SEQ * c + SEQ], w[:, k, P * ch:P * ch + P], rhs[:, k, :],
                                 start=(k == 0), stop=(k == kn - 1), skip_group_check=True)
                end(ins, name)

            for t in range(TT):
                for h in range(2):
                    wait_emptied(pe, f"qT{t}{h}")
                wait_emptied(pe, f"kT{t}")
            for name in _steps:
                if name.startswith("mp"):
                    h = int(name[2:])
                    pe.wait_ge(mprob_ready, h + 1)
                    transposes(name, [mprob[:, h % 2, t, P * kb:P * kb + P] for kb in range(2) for t in range(TT)])
                elif name.startswith("mo"):
                    g = int(name[2:])
                    o = begin(name)
                    for h in (2 * g, 2 * g + 1):
                        wait_emptied(pe, f"mp{h}")
                        for kb in range(2):
                            ins = mm(o[:, SEQ * (h % 2):SEQ * (h % 2) + SEQ], mv_tm[:, kb, P * h:P * h + P],
                                     mpT[:, h % 2, kb, :], start=(kb == 0), stop=(kb == 1), skip_group_check=True)
                    end(ins, name)
                elif name.startswith("gate"):
                    n = int(name[4:])
                    w = wait_block(f"gate{n // 2}").rearrange("p (k n) -> p k n", k=KD)
                    channel_major(name, w, hT, (2 * (n % 2), 2 * (n % 2) + 1), KD)
                elif name.startswith("pv"):
                    j = int(name[2:])
                    for h in range(4 * j, 4 * j + 4):
                        wait_emptied(pe, f"p{h}")
                    weighted_values(j)
                elif name.startswith("p"):
                    h = int(name[1:])
                    pe.wait_ge(prob_ready, h + 1)
                    transposes(name, [prob[:, h % 4, P * b:P * b + P] for b in range(3)])
                else:
                    scores(int(name[1:]))
            pe.wait_ge(gelu_done, 1)
            for t in range(TT):
                transposes(f"gT{t}", [y_tm[:, t, P * k:P * k + P] for k in range(4)])
            for t in range(TT):
                wait_emptied(pe, f"gT{t}")
            w = wait_block("glu")
            for i, name in enumerate(("gv", "gg")):
                wi = w[:, 2048 * i:2048 * i + 2048].rearrange("p (k n) -> p k n", k=4)
                for n in range(2):
                    channel_major(f"{name}{n}", wi, gT, (2 * n, 2 * n + 1), 4)
            for j in range(4):
                wait_emptied(pe, f"pv{j}")
            for i in range(4):
                w = wait_block(f"swa{i // 2}").rearrange("p (k n) -> p k n", k=KD)
                channel_major(f"br1{i}", w, y_swaT, (2 * (i % 2), 2 * (i % 2) + 1), KD)
            for n in range(2):
                wait_emptied(pe, f"gv{n}")
            for i in range(4):
                w = wait_block("ssm").rearrange("p (k n) -> p k n", k=4)
                channel_major(f"br0{i}", w, y_ssmT, (2 * i, 2 * i + 1), 4)
            for j in range(2):
                wait_emptied(pe, f"mo{j}")
            for i in range(4):
                w = wait_block("mem").rearrange("p (k n) -> p k n", k=4)
                channel_major(f"br2{i}", w, y_memT, (2 * i, 2 * i + 1), 4)
            pe.wait_ge(merged_ready, 4)
            for n in range(2):
                for t in range(TT):
                    w = wait_block(f"out{n}").rearrange("p (k n) -> p k n", k=KD)
                    o = begin(f"o{t}{n}")
                    for k in range(KD):
                        ins = mm(o, merged[:, k, P * t:P * t + P], w[:, k, :], start=(k == 0), stop=(k == KD - 1))
                    end(ins, f"o{t}{n}")
            for t in range(TT):
                pe.wait_ge(h2_ready, 2 + t)
                for h in range(2):
                    transposes(f"hT{t}{h}", [h2[:, t, P * k:P * k + P] for k in range(4 * h, 4 * h + 4)])
            for t in range(TT):
                for h in range(2):
                    wait_emptied(pe, f"hT{t}{h}")
            pe.wait_ge(router_in, 32)
            o = begin("logit")
            for t in range(TT):
                for k in range(KD):
                    ins = mm(o[:, EXPERTS * t:EXPERTS * t + EXPERTS], h2T[:, k, P * t:P * t + P], wr_sb[:, k, :],
                             start=(k == 0), stop=(k == KD - 1), skip_group_check=True)
            end(ins, "logit")
            pe.wait_ge(chosen_ready, 1)
            pe.wait_ge(consts, 3)
            o = begin("pos")
            mm(o[:, 0:32], before_bf[:, :], chosen[:, 0, :], start=True, stop=True, skip_group_check=True)
            mm(o[:, 32:64], before_bf[:, :], chosen[:, 1, :], start=True, stop=False, skip_group_check=True)
            mm(o[:, 32:64], ones_bf[:, :], chosen[:, 0, :], start=False, stop=True, skip_group_check=True)
            mm(o[:, 64:96], ones_bf[:, :], chosen[:, 0, :], start=True, stop=False, skip_group_check=True)
            end(mm(o[:, 64:96], ones_bf[:, :], chosen[:, 1, :], start=False, stop=True, skip_group_check=True), "pos")
            transposes("combT", [comb[:, t, :] for t in range(TT)])
            pe.wait_ge(late_in, 32)
            wait_emptied(pe, "combT")
            for b in range(8):
                pe.wait_ge(bank_free[b], TURNS[b])
            for t in range(TT):
                for n in range(2):
                    ins = mm(acc[t][n], combT[0:EXPERTS, P * t:P * t + P], b2_sb[0:EXPERTS, 512 * n:512 * n + 512],
                             start=True, stop=False, skip_group_check=True)

            def gather(i, n):
                for k in range(4):
                    for t in range(TT):
                        ins = mm(ps[:, TB, P * k:P * k + P], h2[:, t, P * (4 * n + k):P * (4 * n + k) + P],
                                 onehot[:, t, :], start=(t == 0), stop=(t == TT - 1), skip_group_check=True)
                ins.then_inc(gather_full, 1)

            def first_matrix(eg, par, wait_hid):
                if wait_hid:
                    pe.wait_ge(hid_free, eg + (par if par else 0))
                pe.wait_ge(row_ready, eg + (par + 1))
                for n in range(2):
                    for h in range(2):
                        q = 2 * n + h
                        mm(ps[SLOTS * h:SLOTS * h + SLOTS, H0 + n, :], bias_row[:, par, :],
                           b1_sb[:, 512 * q:512 * q + 512], start=True, stop=False, skip_group_check=True)
                for k in range(KD):
                    pe.wait_ge(w1_loaded[k], (eg + (par + 1)) * 16)
                    w = ring[:, k // 2, (k % 2) * 2048:(k % 2) * 2048 + 2048]
                    for n in range(2):
                        for h in range(2):
                            q = 2 * n + h
                            ins = mm(ps[SLOTS * h:SLOTS * h + SLOTS, H0 + n, :],
                                     hgT[:, k, SLOTS * par:SLOTS * par + SLOTS], w[:, 512 * q:512 * q + 512],
                                     start=False, stop=(k == KD - 1), skip_group_check=True)
                    ins.then_inc(w1_used, 1)

            def act_transposes(eg, par, c):
                pe.wait_ge(act_ready, eg + (c + 1))
                for n in range(2):
                    for j in range(2):
                        ins = nc.tensor.transpose(ps[:, TB, P * (2 * n + j):P * (2 * n + j) + P],
                                                  act_sb[:, par, n, P * j:P * j + P], ident[:, :])
                ins.then_inc(actT_full, 1)

            def second_matrix(eg, c):
                pe.wait_ge(actT_ready, eg + (c + 1))
                for r in range(KD):
                    n, h, j = r // 4, r // 2 % 2, r % 2
                    pe.wait_ge(w2_loaded[r], (eg + (c + 1)) * 16)
                    for o in range(2):
                        ins = mm(ps[SLOTS * o:SLOTS * o + SLOTS, YB, :],
                                 actT[:, 2 * n + j, SLOTS * h:SLOTS * h + SLOTS],
                                 w2ring[:, r * D + 512 * o:r * D + 512 * o + 512],
                                 start=(r == 0), stop=(r == KD - 1), skip_group_check=True)
                    ins.then_inc(w2_used, 1)

            def scatter(eg, par, c):
                pe.wait_ge(y_ready, eg + (c + 1))
                for t in range(TT):
                    for h in range(2):
                        ins = mm(acc[t][h], scT[SLOTS * h:SLOTS * h + SLOTS, par, P * t:P * t + P],
                                 y_sb[SLOTS * h:SLOTS * h + SLOTS, :], start=False, stop=False,
                                 skip_group_check=True)
                ins.then_inc(scattered, 1)

            def moe(p, first_pass):
                eg0 = p * EXPERTS
                pe.wait_ge(onehot_ready, p * 16 + 1)
                if not first_pass:
                    pe.wait_ge(actT_ready, eg0)
                gather(p * 16, 0)
                pe.wait_ge(gather_ready, (p * 16) * 2 + 1)
                gather(p * 16, 1)
                pe.wait_ge(gather_ready, (p * 16) * 2 + 2)

                def pair(i, first=False, last=False):
                    e = 2 * i
                    pe.wait_ge(gather_ready, i * 2 + 2)
                    first_matrix(e, 0, not (first and first_pass))
                    if not first:
                        scatter(e, 0, -2)
                        act_transposes(e, 1, -1)
                        second_matrix(e, -1)
                    first_matrix(e, 1, True)
                    if not first:
                        scatter(e, 1, -1)
                    pe.wait_ge(weighted_ready, i + 1)
                    if not first:
                        pe.wait_ge(actT_ready, e)
                    for a in range(2):
                        for t in range(TT):
                            ins = nc.tensor.transpose(ps[:, TB, SEQ * a + P * t:SEQ * a + P * t + P],
                                                      onehot_w[:, a, t, :], ident[:, :])
                    ins.then_inc(scT_full, 1)
                    pe.wait_ge(scT_ready, i + 1)
                    if not last:
                        pe.wait_ge(onehot_ready, i + 2)
                        gather(i + 1, 0)
                        pe.wait_ge(gather_ready, i * 2 + 3)
                    act_transposes(e, 0, 0)
                    pe.wait_ge(actT_ready, e + 1)
                    if not last:
                        gather(i + 1, 1)
                    second_matrix(e, 0)

                pair(p * 16, first=True)
                with pe.Fori(1, 15) as i:
                    pair(i + p * 16)
                pair(p * 16 + 15, last=True)
                scatter(eg0, 0, EXPERTS - 2)
                act_transposes(eg0, 1, EXPERTS - 1)
                second_matrix(eg0, EXPERTS - 1)
                scatter(eg0, 1, EXPERTS - 1)

            moe(0, True)
            pe.wait_ge(count_ready, 1)
            most = pe.value_load(count[0:1, 0:1], min_val=0, max_val=SEQ)
            with pe.Fori(1, PASSES) as p:
                with pe.If(most > p * SLOTS):
                    moe(p, False)
            pe.drain().then_inc(acc_full, 1)

        @block.vector
        def _(dve):
            steps = [0]
            V = nc.vector

            def link(ins, s=None, n=None):
                if s is None:
                    steps[0] += 1
                    s, n = dve_step, steps[0]
                ins.then_inc(s, 1)
                dve.wait_ge(s, n)

            def free(ins, name):
                link(ins, bank_free[BANK[name]], TURN[name])

            dve.wait_ge(ldt_in, 16)
            V.tensor_copy(prm[32:48, :].rearrange("q (h s) -> q h s", h=2),
                          ldt_raw[32:48, :].unsqueeze(2).broadcast_to([PAIRS, 2, STATE])).then_inc(ldt_ready, 1)
            for i, (src, dst, g, arrived, ready) in enumerate((
                    (xres, h_tm, g_attn, gx_in, h_ready), (mem_tm, mem_tm, g_mem, gm_in, mem_ready))):
                dve.wait_ge(rstd_done, i + 1)
                dve.wait_ge(arrived, 16)
                for t in range(TT):
                    V.scalar_tensor_tensor(dst[:, t, :], src[:, t, :], ss[:, 2 * i + t:2 * i + t + 1], g,
                                           op0=ALU.mult, op1=ALU.mult).then_inc(ready, 1)

            T = [tb[:, i, :] for i in range(26)]

            def tt(o, a, b, op):
                link(V.tensor_tensor(o, a, b, op))

            def tsc(o, a, s1, op0, s2=None, op1=None):
                if s2 is None:
                    link(V.tensor_scalar(o, a, s1, None, op0))
                else:
                    link(V.tensor_scalar(o, a, s1, s2, op0, op1))

            def stt(o, a, s, b, op0, op1):
                link(V.scalar_tensor_tensor(o, a, s, b, op0=op0, op1=op1))

            def reduce_angle(r, x, q):
                tsc(q, x, 1.0 / (2 * np.pi), ALU.mult, MAGIC, ALU.add)
                tsc(q, q, MAGIC, ALU.subtract)
                stt(r, q, -TWO_PI[0], x, ALU.mult, ALU.add)
                stt(r, q, -TWO_PI[1], r, ALU.mult, ALU.add)
                stt(r, q, -TWO_PI[2], r, ALU.mult, ALU.add)
                tsc(r, r, PI_BOUND, ALU.min, -PI_BOUND, ALU.max)

            wait_emptied(dve, "param")
            a_re, a_im, ldt = prmT[:, 0:16], prmT[:, 16:32], prmT[:, 32:48]
            x_, q_, r_, p_, dt_ = T[0], T[1], T[2], T[3], T[4]
            tsc(x_, ldt, 88.0, ALU.min, -87.0, ALU.max)
            tsc(q_, x_, float(1 / np.log(2)), ALU.mult, MAGIC, ALU.add)
            tsc(q_, q_, MAGIC, ALU.subtract)
            stt(r_, q_, -LN2[0], x_, ALU.mult, ALU.add)
            stt(r_, q_, -LN2[1], r_, ALU.mult, ALU.add)
            tsc(p_, r_, 1 / 5040., ALU.mult)
            for c in (1 / 720., 1 / 120., 1 / 24., 1 / 6., 0.5, 1.0):
                stt(p_, p_, c, r_, ALU.add, ALU.mult)
            tsc(p_, p_, 1.0, ALU.add)
            link(V.tensor_scalar(tbi[:, :], q_, 127.0, 2.0 ** 23, ALU.add, ALU.mult))
            tt(dt_, p_, tbi[:, :].bitcast(F32), ALU.mult)
            re_, im_, th = T[5], a_im, T[6]
            tsc(re_, a_re, -1e-4, ALU.min)
            tt(th, im_, dt_, ALU.mult)
            reduce_angle(T[8], th, q_)
            tsc(T[9], T[8], 0.5, ALU.mult)
            link(V.tensor_copy(q_, T[9]), angle_ready, 1)
            E = T[7]
            tt(x_, re_, dt_, ALU.mult)
            tsc(x_, x_, -88.0, ALU.max, 1 / 128., ALU.mult)
            tsc(E, x_, 1 / 5040., ALU.mult)
            for c in (1 / 720., 1 / 120., 1 / 24., 1 / 6., 0.5, 1.0):
                stt(E, E, c, x_, ALU.add, ALU.mult)
            for _ in range(7):
                stt(E, E, 2.0, E, ALU.add, ALU.mult)
            dve.wait_ge(sin_done, 1)
            sn, hf = T[10], T[11]
            cos_, am_re, am_im = T[12], T[13], T[14]
            tt(q_, hf, hf, ALU.mult)
            tsc(cos_, q_, -2.0, ALU.mult, 1.0, ALU.add)
            tt(am_re, E, cos_, ALU.mult)
            stt(am_re, q_, -2.0, am_re, ALU.mult, ALU.add)
            stt(am_im, E, 1.0, sn, ALU.add, ALU.mult)
            link(V.memset(pw_re[:, 0, :], 1.0))
            link(V.memset(pw_im[:, 0, :], 0.0))
            stt(pw_re[:, 1, :], E, 1.0, cos_, ALU.add, ALU.mult)
            link(V.tensor_copy(pw_im[:, 1, :], am_im))
            t0, t1 = T[16:20], T[20:24]
            for n in (1, 2, 4):
                s0, s1 = tb[:, 16:16 + n, :], tb[:, 20:20 + n, :]
                lo = slice(1, 1 + n)
                hi = slice(1 + n, 1 + 2 * n)
                br = pw_re[:, n, :].unsqueeze(1).broadcast_to([P, n, PAIRS])
                bi = pw_im[:, n, :].unsqueeze(1).broadcast_to([P, n, PAIRS])
                tt(s0, pw_re[:, lo, :], br, ALU.mult)
                tt(s1, pw_im[:, lo, :], bi, ALU.mult)
                tt(pw_re[:, hi, :], s0, s1, ALU.subtract)
                tt(s0, pw_re[:, lo, :], bi, ALU.mult)
                tt(s1, pw_im[:, lo, :], br, ALU.mult)
                tt(pw_im[:, hi, :], s0, s1, ALU.add)
            d_, f_re, f_im = T[15], T[16], T[17]
            tt(T[18], re_, re_, ALU.mult)
            tt(T[19], im_, im_, ALU.mult)
            tt(d_, T[18], T[19], ALU.add)
            link(V.reciprocal(d_, d_))
            tt(T[18], am_re, re_, ALU.mult)
            tt(T[19], am_im, im_, ALU.mult)
            tt(T[18], T[18], T[19], ALU.add)
            tt(f_re, T[18], d_, ALU.mult)
            tt(T[18], am_im, re_, ALU.mult)
            tt(T[19], am_re, im_, ALU.mult)
            tt(T[18], T[18], T[19], ALU.subtract)
            tt(f_im, T[18], d_, ALU.mult)
            dve.wait_ge(bc_in, 64)
            fr = f_re.unsqueeze(2).broadcast_to([P, PAIRS, GCH])
            fi = f_im.unsqueeze(2).broadcast_to([P, PAIRS, GCH])
            tmp = sq[:, 0:256].rearrange("p (q c) -> p q c", q=PAIRS)
            tt(bb_re, b_re, fr, ALU.mult)
            tt(tmp, b_im, fi, ALU.mult)
            tt(bb_re, bb_re, tmp, ALU.subtract)
            tt(bb_im, b_im, fr, ALU.mult)
            tt(tmp, b_re, fi, ALU.mult)
            link(V.tensor_tensor(bb_im, bb_im, tmp, ALU.add), powers_ready, 1)
            for i in range(2):
                link(V.tensor_copy(a8[:, 0, i, :], pw_re[:, CHUNK, :]))
            tsc(a8[:, 1, 0, :], pw_im[:, CHUNK, :], -1.0, ALU.mult)
            link(V.tensor_copy(a8[:, 1, 1, :], pw_im[:, CHUNK, :]))
            wait_emptied(dve, "cparam")
            full = [P, PAIRS, CHUNK + 1, GCH]
            cr, ci = (v.unsqueeze(2).broadcast_to(full) for v in (c_re, c_im))
            pr, pi = (v[:, :, :].rearrange("p t q -> p q t").unsqueeze(3).broadcast_to(full) for v in (pw_re, pw_im))
            tt(ca_re, cr, pr, ALU.mult)
            tt(ca_tmp, ci, pi, ALU.mult)
            tt(ca_re, ca_re, ca_tmp, ALU.subtract)
            tt(ca_im, cr, pi, ALU.mult)
            tt(ca_tmp, ci, pr, ALU.mult)
            tt(ca_im, ca_im, ca_tmp, ALU.add)
            link(V.tensor_scalar(ca_im, ca_im, -1.0, None, ALU.mult), ca_ready, 1)

            dve.wait_ge(small_in, 80)
            dve.wait_ge(consts, 6)
            link(V.tensor_copy(posf[:, :], posi[:, :]))
            for t in range(TT):
                tsc(rope[:, 4, t, :], freq[:, :], posf[:, t:t + 1], ALU.mult)
            flat = [rope[:, i, :, :].rearrange("p t f -> p (t f)") for i in range(6)]
            reduce_angle(flat[0], flat[4], flat[5])
            link(V.tensor_scalar(flat[1], flat[0], 0.5, None, ALU.mult), angle_ready, 2)
            dve.wait_ge(sin_done, 2)
            tt(flat[5], flat[3], flat[3], ALU.mult)
            tsc(flat[3], flat[5], -2.0, ALU.mult, 1.0, ALU.add)

            asked = [0]

            def sums(v, heads, width):
                i = asked[0]
                s = sq[:, 0:heads * width].rearrange("p (h d) -> p h d", h=heads)
                tt(s, v, v, ALU.mult)
                asked[0] += 1
                link(V.tensor_reduce(hs[:, i, 0:heads], s, AX.X, ALU.add), rstd_asked, i + 1)
                return hs[:, i, 0:heads]

            def normed(v, r, i, heads, width):
                dve.wait_ge(rstd_done, 2 + i + 1)
                return V.tensor_tensor(v, v, r.unsqueeze(2).broadcast_to([P, heads, width]), ALU.mult)

            def rotate(v, t, heads, dst):
                sh = [P, heads, ROPE_HALF]
                a = [rtmp[:, i, 0:heads * ROPE_HALF].rearrange("p (h f) -> p h f", h=heads) for i in range(4)]
                s = rope[:, 2, t, :].unsqueeze(1).broadcast_to(sh)
                c = rope[:, 3, t, :].unsqueeze(1).broadcast_to(sh)
                t1, t2 = v[:, :, 0:ROPE_HALF], v[:, :, ROPE_HALF:2 * ROPE_HALF]
                tt(a[0], t1, c, ALU.mult)
                tt(a[1], t2, s, ALU.mult)
                tt(a[2], t2, c, ALU.mult)
                tt(a[3], t1, s, ALU.mult)
                tt(dst[:, :, 0:ROPE_HALF], a[0], a[1], ALU.subtract)
                return V.tensor_tensor(dst[:, :, ROPE_HALF:2 * ROPE_HALF], a[2], a[3], ALU.add)

            for n in range(2):
                for t in range(TT):
                    wait_emptied(dve, f"q{n}{t}")
            heads8 = [(t, q_tm[:, t, 512 * n:512 * n + 512].rearrange("p (h d) -> p h d", h=8))
                      for n in range(2) for t in range(TT)]
            r_of = [sums(v, 8, HD) for _, v in heads8]
            for t in range(TT):
                wait_emptied(dve, f"kv{t}")
            keys = [kv_tm[:, t, 0:256].rearrange("p (h d) -> p h d", h=KVH) for t in range(TT)]
            r_of += [sums(v, KVH, HD) for v in keys]
            for i, (t, v) in enumerate(heads8):
                link(normed(v, r_of[i], i, 8, HD))
                tt(v, v, gain_q[:, :].unsqueeze(1).broadcast_to([P, 8, HD]), ALU.mult)
                link(rotate(v, t, 8, v), qk_ready, i + 1)
            for t, v in enumerate(keys):
                link(normed(v, r_of[4 + t], 4 + t, KVH, HD))
                tt(v, v, gain_k[:, :].unsqueeze(1).broadcast_to([P, KVH, HD]), ALU.mult)
                link(rotate(v, t, KVH, v))
                link(V.tensor_copy(kdup[:, t, :, 0, :], v))
                link(V.tensor_copy(kdup[:, t, :, 1, :], v), qk_ready, 5 + t)
            for t in range(TT):
                wait_emptied(dve, f"qm{t}")
                wait_emptied(dve, f"mk{t}")
            mems = [v[:, t, :].rearrange("p (h d) -> p h d", h=MH) for v in (qm_tm, mk_tm) for t in range(TT)]
            r_of = [sums(v, MH, MHD) for v in mems]
            for i, v in enumerate(mems):
                link(normed(v, r_of[i], 6 + i, MH, MHD), qk_ready, 7 + i)

            wait_full(dve, "xre")
            wait_full(dve, "xim")
            wait_emptied(dve, "lag0")
            wait_emptied(dve, "lag1")
            dve.wait_ge(toep_in, 32 * 16)
            link(V.memset(st[:, :, :, 0], 0.0))
            xs = [bank(n).rearrange("p (q k) -> p q k", q=PAIRS) for n in ("xre", "xim")]
            for k in range(NCHUNK - 1):
                tt(stp[:, 0], st[:, :, :, k], a8[:, 0], ALU.mult)
                tt(stp[:, 1], st[:, ::-1, :, k], a8[:, 1], ALU.mult)
                tt(stp[:, 0], stp[:, 0], stp[:, 1], ALU.add)
                for i in range(2):
                    ins = V.tensor_tensor(st[:, i, :, k + 1], stp[:, 0, i, :], xs[i][:, :, k], ALU.add)
                    if k == NCHUNK - 2:
                        free(ins, ("xre", "xim")[i])
                    else:
                        link(ins)
            V.tensor_copy(stp[:, 0, :, :], stp[:, 0, :, :]).then_inc(scan_done, 1)

            def mem_max(h):
                wait_full(dve, f"ms{h}")
                v = bank(f"ms{h}").rearrange("p (t n) -> p t n", t=TT)
                link(V.tensor_reduce(msm[:, 0, :, h], v, AX.X, ALU.max))
                V.tensor_scalar(msm[:, 1, :, h], msm[:, 0, :, h], -MHD ** -0.5, None, ALU.mult)\
                    .then_inc(mmax_ready, 1)

            def mem_scale(h):
                wait_emptied(dve, f"ms{h}")
                link(V.reciprocal(msm[:, 3, :, h], msm[:, 2, :, h]))
                for t in range(TT):
                    ins = V.tensor_scalar(mprob[:, h % 2, t, :], mprob[:, h % 2, t, :], msm[:, 3, t, h:h + 1],
                                          None, ALU.mult)
                    if t == 0:
                        link(ins)
                ins.then_inc(mprob_ready, 1)

            def swa_max(h):
                wait_full(dve, f"s{h}")
                if h >= 4:
                    wait_full(dve, f"p{h - 4}")
                s = prob[:, h % 4, :]
                free(V.scalar_tensor_tensor(s, bank(f"s{h}")[:, 0:3 * P], HD ** -0.5, mask[:, :],
                                            op0=ALU.mult, op1=ALU.add), f"s{h}")
                link(V.tensor_reduce(smx[:, 0, h:h + 1], s[:, 0:P], AX.X, ALU.max))
                link(V.tensor_reduce(smx[:, 1, h:h + 1], s[:, P:3 * P], AX.X, ALU.max))
                V.tensor_scalar(snm[:, :, h], smx[:, :, h], sink[:, h:h + 1], -1.0, ALU.max, ALU.mult)\
                    .then_inc(smax_ready, 1)

            def swa_scale(h):
                dve.wait_ge(exp_done, 3 * h + 3)
                s = prob[:, h % 4, :]
                tt(sden[:, :, h], sden[:, :, h], ses[:, :, h], ALU.add)
                link(V.reciprocal(sden[:, :, h], sden[:, :, h]))
                link(V.tensor_scalar(s[:, 0:P], s[:, 0:P], sden[:, 0, h:h + 1], None, ALU.mult))
                V.tensor_scalar(s[:, P:3 * P], s[:, P:3 * P], sden[:, 1, h:h + 1], None, ALU.mult)\
                    .then_inc(prob_ready, 1)

            dve.wait_ge(consts, 2)
            dve.wait_ge(y8_out, 32)
            for h in range(MH):
                mem_max(h)
            for h in range(HEADS + 1):
                if h < HEADS:
                    swa_max(h)
                if h < MH:
                    mem_scale(h)
                if h >= 1:
                    swa_scale(h - 1)
            dve.wait_ge(d_in, 16)
            for t in range(TT):
                tt(sq[:, :], u_tm[:, t, :], d_bc[:, :], ALU.mult)
                ins = V.tensor_tensor(y_tm[:, t, :], y_tm[:, t, :], sq[:, :], ALU.add)
                if t == 0:
                    link(ins)
            link(ins, y_skip, 1)
            for n in range(2):
                wait_full(dve, f"gv{n}")
                wait_emptied(dve, f"gg{n}")
                ins = V.tensor_tensor(y_ssmT[:, 2 * n:2 * n + 2, :].rearrange("p a b -> p (a b)"),
                                      bank(f"gv{n}"), sq[:, :], ALU.mult)
                free(ins, f"gv{n}")

            for b in (1, 0, 2):
                for i in range(4):
                    wait_full(dve, f"br{b}{i}")
                    if b == 1 and i == 0:
                        for g in range(12):
                            wait_emptied(dve, f"gate{g}")
                        for h in range(12, HEADS):
                            wait_full(dve, f"p{h}")
                        wait_full(dve, "mp3")
                    g = gates[:, 8 * b + 2 * i:8 * b + 2 * i + 2, :].rearrange("p a b -> p (a b)")
                    m = merged[:, 2 * i:2 * i + 2, :].rearrange("p a b -> p (a b)")
                    if b == 1:
                        free(V.tensor_tensor(m, bank(f"br{b}{i}"), g, ALU.mult), f"br{b}{i}")
                        continue
                    free(V.tensor_tensor(sq[:, :], bank(f"br{b}{i}"), g, ALU.mult), f"br{b}{i}")
                    if b == 2:
                        link(V.tensor_tensor(m, m, sq[:, :], ALU.add), merged_ready, i + 1)
                    else:
                        tt(m, m, sq[:, :], ALU.add)
            for t in range(TT):
                for n in range(2):
                    wait_full(dve, f"o{t}{n}")
                    v = xres[:, t, 512 * n:512 * n + 512]
                    free(V.tensor_tensor(v, bank(f"o{t}{n}"), v, ALU.add), f"o{t}{n}")
            link(V.tensor_copy(cmax[:, :], xres[:, 0, 0:1]), h2_ready, 1)
            dve.wait_ge(rstd_done, 13)
            dve.wait_ge(gf_in, 16)
            for t in range(TT):
                link(V.scalar_tensor_tensor(h2[:, t, :], xres[:, t, :], ss[:, t:t + 1], g_ffn,
                                            op0=ALU.mult, op1=ALU.mult), h2_ready, 2 + t)
            wait_full(dve, "logit")
            dve.wait_ge(router_in, 32)
            o = bank("logit")[:, 0:2 * EXPERTS].rearrange("p (t e) -> p t e", t=TT)
            free(V.tensor_tensor(lg[:, :, :], o, br_bc[:, :].unsqueeze(1).broadcast_to([P, TT, EXPERTS]),
                                 ALU.add), "logit")
            for t in range(TT):
                link(V.max(top[:, t, :], lg[:, t, :]))
                link(V.max_index(topi[:, t, :], top[:, t, :], lg[:, t, :]))
                tsc(topw[:, t, 4:5], top[:, t, 0:1], -1.0, ALU.mult)
            link(V.tensor_copy(topf[:, :, :], topi[:, :, :]), top_ready, 1)
            dve.wait_ge(topexp_done, 2)
            for t in range(TT):
                link(V.reciprocal(topw[:, t, 6:7], topw[:, t, 5:6]))
                tsc(topw[:, t, 0:TOPK], topw[:, t, 0:TOPK], topw[:, t, 6:7], ALU.mult)
                tsc(comb[:, t, :], iota_e[:, :], topf[:, t, 0:1], ALU.is_equal, topw[:, t, 0:1], ALU.mult)
                for k in range(1, TOPK):
                    tsc(ctmp[:, :], iota_e[:, :], topf[:, t, k:k + 1], ALU.is_equal, topw[:, t, k:k + 1], ALU.mult)
                    tt(comb[:, t, :], comb[:, t, :], ctmp[:, :], ALU.add)
            link(V.tensor_scalar(chosen[:, :, :], comb[:, :, :], 0.0, None, ALU.is_gt), chosen_ready, 1)
            wait_full(dve, "pos")
            o = bank("pos")
            link(V.scalar_tensor_tensor(posm[:, :, :], o[:, 0:64].rearrange("p (t e) -> p t e", t=TT), 1.0,
                                        chosen[:, :, :], op0=ALU.add, op1=ALU.mult))
            tsc(posm[:, :, :], posm[:, :, :], 1.0, ALU.subtract)
            free(V.tensor_reduce(cmax[:, :], o[:, 64:96], AX.X, ALU.max), "pos")
            link(V.tensor_copy(count[:, :], cmax[:, :]), count_ready, 1)

            def one_hots(e, i):
                for a in range(2):
                    for t in range(TT):
                        ins = V.tensor_scalar(onehot[:, t, SLOTS * a:SLOTS * a + SLOTS], iota2[:, 0:SLOTS],
                                              posm[:, t, bass.ds(e + a, 1)], None, ALU.is_equal)
                ins.then_inc(onehot_ready, 1)

            def weighted(e):
                for a in range(2):
                    for t in range(TT):
                        ins = V.tensor_scalar(onehot_w[:, a, t, :], iota2[:, :], posm[:, t, bass.ds(e + a, 1)],
                                              comb[:, t, bass.ds(e + a, 1)], ALU.is_equal, ALU.mult)
                ins.then_inc(weighted_ready, 1)

            def bias_rows(e, par):
                V.tensor_copy(bias_row[:, par, :], ident[:, bass.ds(e + par, 1)].broadcast_to([P, SLOTS]))\
                    .then_inc(row_ready, 1)

            def activation(eg, par, c, first=False):
                if not first:
                    dve.wait_ge(act_ready, eg + c)
                dve.wait_ge(w1_used, (eg + (c + 1)) * KD)
                h = ps[:, H0:H0 + 2, :].rearrange("p b (n two) -> p b n two", two=2)
                V.tensor_scalar(hid_g, h[:, :, :, 0], LIMIT, None, ALU.min).then_inc(glu_in, 1)
                V.tensor_scalar(hid_l, h[:, :, :, 1], LIMIT, -LIMIT, ALU.min, ALU.max).then_inc(hid_free, 1)
                dve.wait_ge(hid_free, eg + (c + 1))
                V.scalar_tensor_tensor(hid_l, hid_l, 1.0, hid_g, op0=ALU.add, op1=ALU.mult).then_inc(moe_dve, 1)
                dve.wait_ge(moe_dve, eg + (c + 1))
                dve.wait_ge(sig_done, eg + (c + 1))
                V.tensor_tensor(act_sb[:, par], hid_l, hid_s, ALU.mult).then_inc(act_ready, 1)

            def moe(p, first_pass):
                eg0 = p * EXPERTS
                if not first_pass:
                    V.tensor_scalar(posm[:, :, :], posm[:, :, :], float(SLOTS), None, ALU.subtract)\
                        .then_inc(pass_step, 1)
                    dve.wait_ge(pass_step, p)
                    dve.wait_ge(gather_full, p * 32)
                one_hots(0, p * 16)

                def pair(e, i, first=False, last=False):
                    if not (first and first_pass):
                        dve.wait_ge(w1_used, i * 16)
                    bias_rows(e, 0)
                    bias_rows(e, 1)
                    if not (first and first_pass):
                        dve.wait_ge(scT_full, i)
                    weighted(e)
                    if not last:
                        dve.wait_ge(gather_full, i * 2 + 2)
                        one_hots(e + 2, i + 1)
                    activation(2 * i, 0, 0, first and first_pass)
                    activation(2 * i, 1, 1)

                pair(0, p * 16, first=True)
                with dve.Fori(1, 15) as i:
                    pair(i * 2, i + p * 16)
                pair(30, p * 16 + 15, last=True)

            moe(0, True)
            dve.wait_ge(count_ready, 1)
            most = dve.value_load(count[0:1, 0:1], min_val=0, max_val=SEQ)
            with dve.Fori(1, PASSES) as p:
                with dve.If(most > p * SLOTS):
                    moe(p, False)
            dve.wait_ge(acc_full, 1)
            for t in range(TT):
                V.tensor_tensor(xres[:, t, :], ps[:, 2 * t:2 * t + 2, :].rearrange("p a b -> p (a b)"),
                                xres[:, t, :], ALU.add).then_inc(out_ready, 1)


_NAMES = ['x', 'mem', 'positions', 'attn_norm_g', 'mem_norm_g', 'w_in', 'b_gate',
          'ssm_log_dt', 'ssm_a_re', 'ssm_a_im', 'ssm_b_re', 'ssm_b_im', 'ssm_c_re', 'ssm_c_im', 'ssm_d',
          'w_glu_v', 'w_glu_g', 'swa_q_gain', 'swa_k_gain', 'swa_sinks',
          'w_mem_kv', 'mem_q_gain', 'mem_k_gain',
          'w_br_ssm', 'w_br_swa', 'w_br_mem', 'w_out',
          'ffn_norm_g', 'w_router', 'b_router', 'w_mlp1', 'b_mlp1', 'w_mlp2', 'b_mlp2']


def kernel(**inputs):
    import concourse.bacc as bacc
    from concourse.bass_utils import run_bass_kernel_spmd

    nc = bacc.Bacc("TRN2", target_bir_lowering=False, num_devices=1)
    arrays, args = {}, []
    for name in _NAMES:
        a = np.ascontiguousarray(np.asarray(inputs[name])[0])
        arrays["in_" + name] = a
        args.append(nc.dram_tensor("in_" + name, a.shape, mybir.dt.from_np(a.dtype), kind="ExternalInput").ap())
    args.append(nc.dram_tensor("layer_out", (SEQ, D), F32, kind="ExternalOutput").ap())
    hybrid_layer(nc, *args)
    r = run_bass_kernel_spmd(nc, [arrays], core_ids=[0])
    return r.results[0]["layer_out"].reshape(1, SEQ, D)
```

```python
from contextlib import ExitStack

import numpy as np
import concourse.bass as bass
import concourse.mybir as mybir
from concourse.alu_op_type import AluOpType as ALU

F32 = mybir.dt.float32
BF16 = mybir.dt.bfloat16
I32 = mybir.dt.int32
U32 = mybir.dt.uint32
ACT = mybir.ActivationFunctionType
AX = mybir.AxisListType

P = 128
D = 1024
SEQ = 256
TT = SEQ // P
KD = D // P
SSM = 512
GROUPS, GCH, STATE = 32, 16, 64
PAIRS = GROUPS // 2
CHUNK = 8
NCHUNK = SEQ // CHUNK
HEADS, KVH, HD = 16, 4, 64
ROPE_HALF = 8
ROPE_THETA = 500000.0
MH, MHD = 4, 128
EXPERTS, TOPK = 32, 4
SLOTS = 64
PASSES = SEQ // SLOTS
FF = 2048
NORM_EPS, QK_EPS = 1e-5, 1e-6
ALPHA, LIMIT = 1.702, 7.0
MAGIC = 1.5 * 2.0 ** 23
TWO_PI = (6.28125, 1.9340515136718750e-03, 1.2556659146e-06)
LN2 = (0.693359375, -2.12194440e-4)
PI_BOUND = 3.1415925
MASKED = -1e30

JOBS = (
    ["param"]
    + [f"xT{t}{h}" for t in range(TT) for h in range(2)]
    + [f"u{t}" for t in range(TT)]
    + ["cparam"]
    + [f"q{n}{t}" for n in range(2) for t in range(TT)]
    + [f"kv{t}" for t in range(TT)]
    + [f"memT{t}{h}" for t in range(TT) for h in range(2)]
    + [f"mk{t}" for t in range(TT)] + [f"mv{t}" for t in range(TT)] + [f"qm{t}" for t in range(TT)]
    + ["lag0", "lag1"] + [f"in{n}" for n in range(8)] + ["uT0", "uT1", "xre", "xim"]
    + [f"qT{t}{h}" for t in range(TT) for h in range(2)] + [f"kT{t}" for t in range(TT)]
    + [f"mkT{t}" for t in range(TT)] + [f"qmT{t}" for t in range(TT)]
)
MEM_STEPS = ["ms0", "ms1", "gate4", "ms2", "ms3", "mp0", "gate5", "mp1", "gate6", "mo0", "mp2", "gate7",
             "mp3", "gate0", "mo1", "gate1"]
SWA_STEPS = []
_fill = {1: ["gate2"], 2: ["gate3"], 3: ["gate8"], 4: ["gate9"], 5: ["gate10"],
         6: ["gate11", "gT0", "gT1"], 7: ["gv0", "gv1"], 8: ["gg0"]}
for _a in range(HEADS // 2 + 1):
    if _a < HEADS // 2:
        SWA_STEPS += [f"s{2 * _a}", f"s{2 * _a + 1}"]
    SWA_STEPS += _fill.get(_a, [])
    if _a in (3, 5, 7):
        SWA_STEPS += [f"pv{(_a - 3) // 2}"]
    if _a >= 1:
        SWA_STEPS += [f"p{2 * _a - 2}", f"p{2 * _a - 1}"]
SWA_STEPS += ["gg1", "pv3"]
JOBS += MEM_STEPS + ["y0", "y1"] + SWA_STEPS
JOBS += [f"br{b}{i}" for b in (1, 0, 2) for i in range(4)]
JOBS += [f"o{t}{n}" for n in range(2) for t in range(TT)]
JOBS += [f"hT{t}{h}" for t in range(TT) for h in range(2)] + ["logit", "pos", "combT"]
BANK = {name: n % 8 for n, name in enumerate(JOBS)}
TURN = {name: n // 8 + 1 for n, name in enumerate(JOBS)}
TURNS = [len([n for n in range(len(JOBS)) if n % 8 == b]) for b in range(8)]

BLOCKS = (["u", "q0", "q1", "kv", "mk", "mv", "qm"] + [f"gate{n}" for n in (2, 3, 0, 1, 4, 5)]
          + ["glu", "swa0", "swa1", "ssm", "mem", "out0", "out1"])
RING = 4
SLOT_OF = {name: n % RING for n, name in enumerate(BLOCKS)}
LOADS_OF = {name: n // RING + 1 for n, name in enumerate(BLOCKS)}
LAST_JOB = {"u": "u1", "q0": "q01", "q1": "q11", "kv": "kv1", "mk": "mk1", "mv": "mv1", "qm": "qm1",
            "glu": "gg1", "swa0": "br11", "swa1": "br13", "ssm": "br03", "mem": "br23",
            "out0": "o10", "out1": "o11"} | {f"gate{n}": f"gate{2 * n + 1}" for n in range(6)}


def hybrid_layer(nc, x, mem, positions, attn_norm_g, mem_norm_g, w_in, b_gate,
                 ssm_log_dt, ssm_a_re, ssm_a_im, ssm_b_re, ssm_b_im, ssm_c_re, ssm_c_im, ssm_d,
                 w_glu_v, w_glu_g, swa_q_gain, swa_k_gain, swa_sinks,
                 w_mem_kv, mem_q_gain, mem_k_gain,
                 w_br_ssm, w_br_swa, w_br_mem, w_out,
                 ffn_norm_g, w_router, b_router, w_mlp1, b_mlp1, w_mlp2, b_mlp2, out):
    ctx = ExitStack()
    with ctx:
        def sb(name, shape, dt=F32):
            return ctx.enter_context(nc.sbuf_tensor(name, shape, dt))

        def sem(name):
            return ctx.enter_context(nc.semaphore(name))

        KB = 256
        ring = sb("ring", [P, RING, 4096])
        w2ring = sb("w2ring", [P, 32 * KB])
        arena = sb("arena", [P, 90 * KB])
        xres = sb("xres", [P, TT, D])

        def at(kb, *dims, base=None):
            size = int(np.prod(dims))
            off = int(kb * KB)
            v = (arena if base is None else base)[:, off:off + size]
            if len(dims) == 2:
                v = v.rearrange("p (a b) -> p a b", a=dims[0])
            if len(dims) == 3:
                v = v.rearrange("p (a b c) -> p a b c", a=dims[0], b=dims[1])
            if len(dims) == 4:
                v = v.rearrange("p (a b c d) -> p a b c d", a=dims[0], b=dims[1], c=dims[2])
            return v

        hT = at(0, KD, SEQ)
        h_tm = at(8, TT, D)
        q_tm = at(8, TT, D)
        mem_tm = at(16, TT, D)
        mk_tm = at(16, TT, 512)
        qm_tm = at(20, TT, 512)
        memT = at(24, KD, SEQ)
        mkT = at(24, MH, SEQ)
        qmT = at(28, MH, SEQ)
        mv_tm = at(32, TT, 512)
        kv_tm = at(36, TT, 512)
        kdup = at(40, TT, KVH, 2, HD)
        u_tm = at(44, TT, SSM)
        y_ssmT = at(44, 4, SEQ)
        y_memT = at(8, MH, SEQ)
        y_swaT = at(16, KD, SEQ)
        gate_at = {n: at(kb, 2, SEQ) for n, kb in zip(
            (4, 5, 6, 7, 0, 1, 2, 3, 8, 9, 10, 11), (82, 84, 86, 88, 66, 68, 48, 50, 52, 54, 56, 58))}
        ca_re = at(48, PAIRS, CHUNK + 1, GCH)
        ca_im = at(57, PAIRS, CHUNK + 1, GCH)
        u8 = at(82, CHUNK, P)
        u8g = at(86, 8, CHUNK, GCH)
        y8 = at(12, CHUNK, P)
        ab_tmp = at(66, PAIRS, CHUNK, GCH)
        b_re, b_im = at(74, PAIRS, GCH), at(75, PAIRS, GCH)
        bb_re, bb_im = at(76, PAIRS, GCH), at(77, PAIRS, GCH)
        c_re, c_im = at(78, PAIRS, GCH), at(79, PAIRS, GCH)
        c_raw = at(80, 2, 2, P)
        g_attn, g_mem = at(82, D), at(86, D)
        uT = at(70, 8, 4, NCHUNK)
        y_tm = at(28, TT, SSM, base=w2ring)
        lag = at(74, 2, 4, P)
        st = at(78, 2, PAIRS, NCHUNK)
        gT = at(12, 4, SEQ)
        ab_re = at(0, PAIRS, CHUNK, GCH, base=w2ring)
        ab_im = at(8, PAIRS, CHUNK, GCH, base=w2ring)
        toep = at(0, 4, 2, 4, P, base=w2ring)
        win_re = at(16, PAIRS, P, base=w2ring)
        win_im = at(24, PAIRS, P, base=w2ring)
        ca_tmp = at(16, PAIRS, CHUNK + 1, GCH, base=w2ring)
        xs = at(28, 2, PAIRS, NCHUNK, base=w2ring)
        pT = at(0, 2, 4, 3, P, base=w2ring)
        mpT = at(74, 2, 2, SEQ)
        qT = at(16, KD, SEQ, base=w2ring)
        kT = at(24, KVH, SEQ, base=w2ring)
        prob = at(60, 4, 3 * P)
        mprob = at(40, 2, TT, SEQ)
        merged = at(72, KD, SEQ)
        d_bc = at(80, SSM)
        wr_sb = at(12, KD, EXPERTS)
        lg = at(13, TT, EXPERTS)
        comb = at(13.25, TT, EXPERTS)
        posm = at(13.5, TT, EXPERTS)
        ctmp = at(13.75, EXPERTS)
        top, topf, topw = at(14, TT, 8), at(14.25, TT, 8), at(14.5, TT, 8)
        h2 = at(0, TT, D)
        h2T = at(72, KD, SEQ)
        onehot = at(8, TT, 2 * SLOTS)
        onehot_w = at(9, 2, TT, 2 * SLOTS)
        bias_row = at(11, 2, SLOTS)
        hid_g, hid_l, hid_s = at(16, 2, 256), at(18, 2, 256), at(20, 2, 256)
        y_sb = at(22, 512)
        hgT = at(24, KD, 2 * SLOTS)
        actT = at(28, 4, P)
        scT = at(30, 2, SEQ)
        act_sb = at(32, 2, 2, 256)
        g_ffn = at(36, D)
        b2_sb = at(40, D)
        combT = at(44, SEQ)
        b1_sb = at(82, FF)

        ident = sb("ident", [P, P])
        ones_bf = sb("ones_bf", [P, P], BF16)
        before_bf = sb("before_bf", [P, P], BF16)
        mask = sb("mask", [P, 3 * P])
        iota2 = sb("iota2", [P, 2 * SLOTS])
        iota_e = sb("iota_e", [P, EXPERTS])
        prm = sb("prm", [74, P])
        ldt_raw = sb("ldt_raw", [48, 2])
        prmT = sb("prmT", [P, 74])
        tb = sb("tb", [P, 26, PAIRS])
        tbi = sb("tbi", [P, PAIRS], I32)
        pw_re = sb("pw_re", [P, CHUNK + 1, PAIRS])
        pw_im = sb("pw_im", [P, CHUNK + 1, PAIRS])
        a8 = sb("a8", [P, 2, 2, PAIRS])
        stp = sb("stp", [P, 2, 2, PAIRS])
        posi = sb("posi", [P, TT], I32)
        posf = sb("posf", [P, TT])
        rope = sb("rope", [P, 6, TT, ROPE_HALF])
        freq = sb("freq", [P, ROPE_HALF])
        gain_q = sb("gain_q", [P, HD])
        gain_k = sb("gain_k", [P, HD])
        sink = sb("sink", [P, HEADS])
        sq = sb("sq", [P, 512])
        rtmp = sq[:, :].rearrange("p (a b) -> p a b", a=4)
        ss = sb("ss", [P, 4])
        hs = sb("hs", [P, 10, 16])
        half = sb("half", [P, 16])
        smx = sb("smx", [P, 2, HEADS])
        snm = sb("snm", [P, 2, HEADS])
        sden = sb("sden", [P, 2, HEADS])
        ses = sb("ses", [P, 2, HEADS])
        msm = sb("msm", [P, 4, TT, MH])
        br_bc = sb("br_bc", [P, EXPERTS])
        topi = sb("topi", [P, TT, 8], U32)
        chosen = sb("chosen", [P, TT, EXPERTS], BF16)
        cmax = sb("cmax", [P, 1])
        count = sb("count", [P, 1], I32)

        ps = ctx.enter_context(nc.psum_tensor("ps", [P, 8, 512], F32))

        bank_full = [sem(f"bank_full{b}") for b in range(8)]
        bank_free = [sem(f"bank_free{b}") for b in range(8)]
        loaded = [sem(f"loaded{s}") for s in range(RING)]
        x_in, mem_in, gx_in, gm_in = sem("x_in"), sem("mem_in"), sem("gx_in"), sem("gm_in")
        prm_in, bc_in, cr_in, posi_in, small_in, router_in = (
            sem("prm_in"), sem("bc_in"), sem("cr_in"), sem("posi_in"), sem("small_in"), sem("router_in"))
        d_in, ldt_in, ldt_ready = sem("d_in"), sem("ldt_in"), sem("ldt_ready")
        late_in, gf_in = sem("late_in"), sem("gf_in")
        consts = sem("consts")
        sq_done = sem("sq_done")
        rstd_asked, rstd_done = sem("rstd_asked"), sem("rstd_done")
        pool_step = sem("pool_step")
        dve_step = sem("dve_step")
        act_step = sem("act_step")
        h_ready, mem_ready = sem("h_ready"), sem("mem_ready")
        angle_ready, sin_done = sem("angle_ready"), sem("sin_done")
        powers_ready, ab_ready, ca_ready = sem("powers_ready"), sem("ab_ready"), sem("ca_ready")
        toep_clear, toep_in = sem("toep_clear"), sem("toep_in")
        u8g_ready = sem("u8g_ready")
        u8_in, y8_out = sem("u8_in"), sem("y8_out")
        scan_done = sem("scan_done")
        qk_ready = sem("qk_ready")
        smax_ready, exp_done, prob_ready = sem("smax_ready"), sem("exp_done"), sem("prob_ready")
        mmax_ready, mexp_done, mprob_ready = sem("mmax_ready"), sem("mexp_done"), sem("mprob_ready")
        y_skip, gelu_done = sem("y_skip"), sem("gelu_done")
        merged_ready = sem("merged_ready")
        h2_ready, top_ready, topexp_done = sem("h2_ready"), sem("top_ready"), sem("topexp_done")
        chosen_ready, count_ready = sem("chosen_ready"), sem("count_ready")
        b1_clear = sem("b1_clear")
        acc_full = sem("acc_full")
        out_ready, out_done = sem("out_ready"), sem("out_done")
        w1_loaded = [sem(f"w1_loaded{k}") for k in range(KD)]
        w2_loaded = [sem(f"w2_loaded{k}") for k in range(KD)]
        w1_used, w2_used = sem("w1_used"), sem("w2_used")
        hid_free = sem("hid_free")
        glu_in, sig_done, act_ready = sem("glu_in"), sem("sig_done"), sem("act_ready")
        actT_full, actT_ready = sem("actT_full"), sem("actT_ready")
        y_ready = sem("y_ready")
        scattered = sem("scattered")
        gather_full, gather_ready = sem("gather_full"), sem("gather_ready")
        scT_full, scT_ready = sem("scT_full"), sem("scT_ready")
        onehot_ready, weighted_ready, row_ready = (
            sem("onehot_ready"), sem("weighted_ready"), sem("row_ready"))
        moe_dve, pass_step = sem("moe_dve"), sem("pass_step")

        block = ctx.enter_context(nc.Block())

        def bank(name):
            return ps[:, BANK[name], :]

        def wait_full(eng, name):
            eng.wait_ge(bank_full[BANK[name]], TURN[name])

        def wait_emptied(eng, name):
            eng.wait_ge(bank_free[BANK[name]], TURN[name])

        acc = [[ps[:, 2 * t + n, :] for n in range(2)] for t in range(TT)]
        H0, YB, TB = 4, 6, 7

        @block.sync
        def _(sp):
            win = w_in.rearrange("(k p) n -> p k n", p=P)
            wkv = w_mem_kv.rearrange("(k p) n -> p k n", p=P)
            wsw = w_br_swa.rearrange("(k p) n -> p k n", p=P)
            wo = w_out.rearrange("(k p) n -> p k n", p=P)

            def load_block(n):
                name = BLOCKS[n]
                if n >= RING:
                    wait_full(sp, LAST_JOB[BLOCKS[n - RING]])
                slot = ring[:, n % RING, :]
                slot8 = slot.rearrange("p (k n) -> p k n", k=KD)
                if name == "glu":
                    for i, w in enumerate((w_glu_v, w_glu_g)):
                        sp.dma_start(slot[:, i * 2048:(i + 1) * 2048].rearrange("p (k n) -> p k n", k=4),
                                     w.rearrange("(k p) n -> p k n", p=P)).then_inc(loaded[n % RING], 8 * 2)
                    return
                if name in ("ssm", "mem"):
                    src = (w_br_ssm if name == "ssm" else w_br_mem).rearrange("(k p) n -> p k n", p=P)
                    sp.dma_start(slot.rearrange("p (k n) -> p k n", k=4), src).then_inc(loaded[n % RING], 16)
                    return
                col = {"u": 0, "q0": 512, "q1": 1024, "kv": 1536, "qm": 2048}
                if name in col:
                    src = win[:, :, col[name]:col[name] + 512]
                elif name.startswith("gate"):
                    src = win[:, :, 2560 + 512 * int(name[4:]):3072 + 512 * int(name[4:])]
                elif name in ("mk", "mv"):
                    src = wkv[:, :, 0:512] if name == "mk" else wkv[:, :, 512:1024]
                else:
                    n0 = 512 * int(name[-1])
                    src = (wsw if name.startswith("swa") else wo)[:, :, n0:n0 + 512]
                sp.dma_start(slot8, src).then_inc(loaded[n % RING], 16)

            sp.dma_start(xres[:, :, :], x.rearrange("(t p) n -> p t n", p=P)).then_inc(x_in, 16)
            sp.dma_start(g_attn, attn_norm_g.unsqueeze(0).broadcast_to([P, D])).then_inc(gx_in, 16)
            load_block(0)
            for t in range(TT):
                sp.dma_start(posi[:, t:t + 1], positions[P * t:P * t + P].unsqueeze(1)).then_inc(posi_in, 16)
            for v, dst in ((ssm_b_re, b_re), (ssm_b_im, b_im)):
                for h in range(2):
                    sp.dma_start(dst[STATE * h:STATE * h + STATE, :, :],
                                 v.rearrange("(q h) s c -> h s q c", h=2)[h]).then_inc(bc_in, 16)
            sp.dma_start(mem_tm, mem.rearrange("(t p) n -> p t n", p=P)).then_inc(mem_in, 16)
            sp.dma_start(g_mem, mem_norm_g.unsqueeze(0).broadcast_to([P, D])).then_inc(gm_in, 16)
            load_block(1)
            for i, v in enumerate((ssm_c_re, ssm_c_im)):
                for r in range(2):
                    src = v.rearrange("(r q h) c s -> r h q c s", r=2, h=2)[r]
                    for h in range(2):
                        sp.dma_start(c_raw[:, i, r, STATE * h:STATE * h + STATE], src[h]).then_inc(cr_in, 16)
            load_block(2)
            load_block(3)
            for v, dst in ((swa_q_gain, gain_q), (swa_k_gain, gain_k), (swa_sinks, sink)):
                sp.dma_start(dst[:, :], v.unsqueeze(0).broadcast_to(dst.shape)).then_inc(small_in, 16)
            sp.dma_start(br_bc[:, :], b_router.unsqueeze(0).broadcast_to([P, EXPERTS])).then_inc(router_in, 16)
            wait_emptied(sp, "u0")
            wait_emptied(sp, "u1")
            sp.wait_ge(h_ready, TT)
            for r in range(4):
                for t in range(TT):
                    lo = 32 * r + 16 * t
                    sp.dma_start(u8[lo:lo + 16, :, :], u_tm[:, t, P * r:P * r + P]).then_inc(u8_in, 16)
            for n in range(4, 10):
                load_block(n)
            sp.wait_ge(toep_clear, 1)
            wait_emptied(sp, "lag0")
            wait_emptied(sp, "lag1")
            for t in range(CHUNK):
                w = P - GCH * t
                for j in range(4):
                    sp.dma_start(toep[GCH * t:GCH * t + GCH, j, :, :, GCH * t:P],
                                 lag[32 * j:32 * j + GCH, :, :, 0:w]).then_inc(toep_in, 16)
            load_block(10)
            wait_emptied(sp, "y0")
            wait_emptied(sp, "y1")
            for r in range(4):
                for t in range(TT):
                    lo = 32 * r + 16 * t
                    sp.dma_start(y_tm[:, t, P * r:P * r + P], y8[lo:lo + 16, :, :]).then_inc(y8_out, 16)
            sp.dma_start(d_bc, ssm_d.unsqueeze(0).broadcast_to([P, SSM])).then_inc(d_in, 16)
            for n in range(11, 17):
                load_block(n)
            wait_full(sp, "mp3")
            sp.dma_start(b2_sb[0:EXPERTS, :], b_mlp2).then_inc(late_in, 16)
            wait_full(sp, "gg1")
            sp.dma_start(wr_sb, w_router.rearrange("(k p) n -> p k n", p=P)).then_inc(router_in, 16)
            load_block(17)
            wait_full(sp, "pv3")
            sp.dma_start(g_ffn, ffn_norm_g.unsqueeze(0).broadcast_to([P, D])).then_inc(gf_in, 16)
            for k in range(KD):
                sp.dma_start(w2ring[:, k * D:(k + 1) * D],
                             w_mlp2[0, P * k:P * k + P, :]).then_inc(w2_loaded[k], 16)
            for n in range(18, len(BLOCKS)):
                load_block(n)

            def load_experts(p):
                w1v = w_mlp1.rearrange("e (k p) n -> e k p n", p=P)
                w2v = w_mlp2.rearrange("e (k p) n -> e k p n", p=P)

                def first_matrix(e, first):
                    for k in range(KD):
                        if first:
                            wait_full(sp, LAST_JOB[BLOCKS[len(BLOCKS) - RING + k // 2]])
                        else:
                            sp.wait_ge(w1_used, (e + EXPERTS * p) * KD + (k + 1 - KD))
                        sp.dma_start(ring[:, k // 2, (k % 2) * 2048:(k % 2) * 2048 + 2048],
                                     w1v[e, k]).then_inc(w1_loaded[k], 16)

                def second_matrix(e):
                    for k in range(KD):
                        sp.wait_ge(w2_used, (e + EXPERTS * p) * KD + (k + 1 - KD))
                        sp.dma_start(w2ring[:, k * D:(k + 1) * D], w2v[e, k]).then_inc(w2_loaded[k], 16)

                return first_matrix, second_matrix

            first_matrix, second_matrix = load_experts(0)
            sp.wait_ge(b1_clear, 1)
            sp.dma_start(b1_sb[0:EXPERTS, :], b_mlp1).then_inc(late_in, 16)
            first_matrix(0, True)
            first_matrix(1, False)
            with sp.Fori(1, EXPERTS - 1) as e:
                first_matrix(e + 1, False)
                second_matrix(e)
            second_matrix(EXPERTS - 1)
            sp.wait_ge(count_ready, 1)
            most = sp.value_load(count[0:1, 0:1], min_val=0, max_val=SEQ)
            with sp.Fori(1, PASSES) as p:
                with sp.If(most > p * SLOTS):
                    first_matrix, second_matrix = load_experts(p)
                    first_matrix(0, False)
                    with sp.Fori(0, EXPERTS - 1) as e:
                        first_matrix(e + 1, False)
                        second_matrix(e)
                    second_matrix(EXPERTS - 1)
            sp.wait_ge(out_ready, TT)
            sp.dma_start(out.rearrange("(t p) n -> p t n", p=P), xres[:, :, :]).then_inc(out_done, 16)
            sp.wait_ge(out_done, 16)

        @block.gpsimd
        def _(pool):
            steps = [0]

            def link(ins):
                steps[0] += 1
                ins.then_inc(pool_step, 1)
                pool.wait_ge(pool_step, steps[0])

            def step(ins):
                steps[0] += 1
                ins.then_inc(pool_step, 1)

            link(pool.memset(half[:, :], -0.5))
            link(pool.memset(ident[:, :], 0.0))
            pool.affine_select(out=ident[:, :], in_=ident[:, :], compare_op=ALU.not_equal, fill=1.0,
                               base=0, pattern=[[-1, P]], channel_multiplier=1).then_inc(consts, 1)
            link(pool.memset(mask[:, :], 0.0))
            link(pool.affine_select(out=mask[:, 0:P], in_=mask[:, 0:P], compare_op=ALU.is_ge, fill=MASKED,
                                    base=0, pattern=[[-1, P]], channel_multiplier=1))
            link(pool.affine_select(out=mask[:, P:2 * P], in_=mask[:, P:2 * P], compare_op=ALU.is_gt,
                                    fill=MASKED, base=0, pattern=[[1, P]], channel_multiplier=-1))
            pool.affine_select(out=mask[:, 2 * P:3 * P], in_=mask[:, 2 * P:3 * P], compare_op=ALU.is_ge,
                               fill=MASKED, base=0, pattern=[[-1, P]],
                               channel_multiplier=1).then_inc(consts, 1)
            link(pool.memset(ones_bf[:, :], 1.0))
            link(pool.memset(before_bf[:, :], 1.0))
            pool.affine_select(out=before_bf[:, :], in_=before_bf[:, :], compare_op=ALU.is_gt, fill=0.0,
                               base=0, pattern=[[1, P]], channel_multiplier=-1).then_inc(consts, 1)
            pool.iota(iota2[:, :], pattern=[[0, 2], [1, SLOTS]], base=0, channel_multiplier=0,
                      allow_small_or_imprecise_dtypes=True).then_inc(consts, 1)
            pool.iota(iota_e[:, :], pattern=[[1, EXPERTS]], base=0, channel_multiplier=0,
                      allow_small_or_imprecise_dtypes=True).then_inc(consts, 1)
            for i in range(ROPE_HALF):
                f = float(np.float32(ROPE_THETA ** (-i / ROPE_HALF)))
                last = pool.memset(freq[:, i:i + 1], f)
            last.then_inc(consts, 1)

            def rstd(v, n, width, eps):
                link(pool.tensor_scalar(v, v, 1.0 / width, eps, ALU.mult, ALU.add))
                pool.tensor_tensor(v, v, half[:, 0:n], ALU.pow).then_inc(rstd_done, 1)

            for i in range(2):
                pool.wait_ge(sq_done, 2 * i + 2)
                rstd(ss[:, 2 * i:2 * i + 2], 2, D, NORM_EPS)
            pool.wait_ge(powers_ready, 1)

            def over_t(v):
                return v.unsqueeze(2).broadcast_to([P, PAIRS, CHUNK, GCH])

            def over_c(v):
                return v[:, CHUNK - 1::-1, :].rearrange("p t q -> p q t").unsqueeze(3)\
                    .broadcast_to([P, PAIRS, CHUNK, GCH])

            def table(dst, b0, p0, b1, p1, op):
                link(pool.tensor_tensor(dst, over_t(b0), over_c(p0), ALU.mult))
                link(pool.tensor_tensor(ab_tmp, over_t(b1), over_c(p1), ALU.mult))
                return pool.tensor_tensor(dst, dst, ab_tmp, op)

            link(table(ab_re, bb_re, pw_re, bb_im, pw_im, ALU.subtract))
            table(ab_im, bb_re, pw_im, bb_im, pw_re, ALU.add).then_inc(ab_ready, 1)
            widths = [HD] * 6 + [MHD] * 4
            counts = [8] * 4 + [4] * 6
            for i in range(10):
                pool.wait_ge(rstd_asked, i + 1)
                rstd(hs[:, i, 0:counts[i]], counts[i], widths[i], QK_EPS)
            wait_full(pool, "in7")
            wait_full(pool, "lag1")
            pool.memset(at(0, 4096, base=w2ring), 0.0).then_inc(toep_clear, 1)

            pool.wait_ge(ca_ready, 1)
            link(pool.memset(st[:, :, :, 0], 0.0))
            wait_emptied(pool, "xre")
            wait_emptied(pool, "xim")
            for k in range(NCHUNK - 1):
                step(pool.tensor_tensor(stp[:, 0], st[:, :, :, k], a8[:, 0], ALU.mult))
                link(pool.tensor_tensor(stp[:, 1], st[:, ::-1, :, k], a8[:, 1], ALU.mult))
                link(pool.tensor_tensor(stp[:, 1], stp[:, 1], xs[:, :, :, k], ALU.add))
                ins = pool.tensor_tensor(st[:, :, :, k + 1], stp[:, 0], stp[:, 1], ALU.add)
                if k < NCHUNK - 2:
                    link(ins)
            ins.then_inc(scan_done, 1)
            for i in range(4):
                wait_emptied(pool, f"br1{i}")
            pool.memset(b1_sb, 0.0).then_inc(b1_clear, 1)
            pool.wait_ge(h2_ready, 1)
            pool.wait_ge(sq_done, 6)
            rstd(ss[:, 0:2], 2, D, NORM_EPS)

        @block.scalar
        def _(act):
            def row(v):
                return v.unsqueeze(0)

            for i, v in enumerate((ssm_a_re, ssm_a_im)):
                act.dma_start(prm[16 * i:16 * i + 16, :], v.rearrange("(q h) s -> q (h s)", h=2)).then_inc(prm_in, 16)
            act.dma_start(ldt_raw[32:48, :], ssm_log_dt.rearrange("(q h) -> q h", h=2)).then_inc(ldt_in, 16)
            act.dma_start(prm[48:72, :], b_gate.rearrange("(c p) -> c p", p=P)).then_inc(prm_in, 16)
            act.dma_start(prm[72:73, :], row(mem_q_gain)).then_inc(prm_in, 16)
            act.dma_start(prm[73:74, :], row(mem_k_gain)).then_inc(prm_in, 16)
            def empty(name, dst, src):
                wait_full(act, name)
                nc.scalar.copy(dst, src).then_inc(bank_free[BANK[name]], 1)

            def square(v, n):
                nc.scalar.activation(at(24, D), v, ACT.Square,
                                     accum_out=ss[:, n:n + 1]).then_inc(sq_done, 1)

            act.wait_ge(x_in, 16)
            square(xres[:, 0, :], 0)
            act.wait_ge(sq_done, 1)
            square(xres[:, 1, :], 1)
            wait_full(act, "param")
            nc.scalar.copy(prmT[:, :], bank("param")[:, 0:74]).then_inc(bank_free[BANK["param"]], 1)
            for t in range(TT):
                for h in range(2):
                    empty(f"xT{t}{h}", hT[:, 4 * h:4 * h + 4, P * t:P * t + P],
                          bank(f"xT{t}{h}").rearrange("p (k n) -> p k n", k=4))
            act.wait_ge(angle_ready, 1)
            nc.scalar.activation(tb[:, 10:12, :], tb[:, 8:10, :], ACT.Sin).then_inc(sin_done, 1)
            act.wait_ge(angle_ready, 2)
            nc.scalar.activation(rope[:, 2:4, :, :], rope[:, 0:2, :, :], ACT.Sin).then_inc(sin_done, 1)
            act.wait_ge(mem_in, 16)
            for t in range(TT):
                act.wait_ge(sq_done, 2 + t)
                square(mem_tm[:, t, :], 2 + t)
            for t in range(TT):
                empty(f"u{t}", u_tm[:, t, :], bank(f"u{t}"))
            wait_full(act, "cparam")
            cp = bank("cparam").rearrange("p (i r n) -> p i (r n)", i=2, r=2)
            nc.scalar.copy(at(78, 2, 256), cp).then_inc(bank_free[BANK["cparam"]], 1)
            for n in range(2):
                for t in range(TT):
                    empty(f"q{n}{t}", q_tm[:, t, 512 * n:512 * n + 512], bank(f"q{n}{t}"))
            for t in range(TT):
                empty(f"kv{t}", kv_tm[:, t, :], bank(f"kv{t}"))
            for t in range(TT):
                for h in range(2):
                    empty(f"memT{t}{h}", memT[:, 4 * h:4 * h + 4, P * t:P * t + P],
                          bank(f"memT{t}{h}").rearrange("p (k n) -> p k n", k=4))
            for t in range(TT):
                empty(f"mk{t}", mk_tm[:, t, :], bank(f"mk{t}"))
            for t in range(TT):
                empty(f"mv{t}", mv_tm[:, t, :], bank(f"mv{t}"))
            for t in range(TT):
                empty(f"qm{t}", qm_tm[:, t, :], bank(f"qm{t}"))
            act.wait_ge(u8_in, 8 * 16)
            act.wait_ge(mem_ready, TT)
            nc.scalar.copy(u8g.rearrange("p g t c -> p t g c"),
                           u8.rearrange("p t (g c) -> p t g c", c=GCH)).then_inc(u8g_ready, 1)
            for h in range(2):
                empty(f"lag{h}", lag[:, h, :, :].rearrange("p s n -> p (s n)"), bank(f"lag{h}"))
            for n in range(8):
                wait_full(act, f"in{n}")
                v = bank(f"in{n}").rearrange("p (q i n) -> p q i n", q=2, i=2)
                nc.scalar.copy(win_re[:, 2 * n:2 * n + 2, :], v[:, :, 0, :]).then_inc(act_step, 1)
                nc.scalar.copy(win_im[:, 2 * n:2 * n + 2, :], v[:, :, 1, :]).then_inc(bank_free[BANK[f"in{n}"]], 1)
            for n in range(2):
                empty(f"uT{n}", uT[:, 4 * n:4 * n + 4, :, :].rearrange("p i r n -> p (i r n)"), bank(f"uT{n}"))
            wait_full(act, "xim")
            for i, name in enumerate(("xre", "xim")):
                empty(name, xs[:, i, :, :].rearrange("p q k -> p (q k)"), bank(name))
            for t in range(TT):
                for h in range(2):
                    empty(f"qT{t}{h}", qT[:, 4 * h:4 * h + 4, P * t:P * t + P],
                          bank(f"qT{t}{h}").rearrange("p (k n) -> p k n", k=4))
            for t in range(TT):
                empty(f"kT{t}", kT[:, :, P * t:P * t + P], bank(f"kT{t}").rearrange("p (k n) -> p k n", k=4))
            for name, dst, col in (("mkT", mkT, 73), ("qmT", qmT, 72)):
                for t in range(TT):
                    wait_full(act, f"{name}{t}")
                    nc.scalar.mul(dst[:, :, P * t:P * t + P],
                                  bank(f"{name}{t}").rearrange("p (k n) -> p k n", k=4),
                                  prmT[:, col:col + 1]).then_inc(bank_free[BANK[f"{name}{t}"]], 1)
            def mem_exp(h):
                act.wait_ge(mmax_ready, h + 1)
                if h >= 2:
                    wait_full(act, f"mp{h - 2}")
                v = bank(f"ms{h}").rearrange("p (t n) -> p t n", t=TT)
                nc.scalar.activation(mprob[:, h % 2, 0, :], v[:, 0, :], ACT.Exp, bias=msm[:, 1, 0, h:h + 1],
                                     scale=MHD ** -0.5, accum_out=msm[:, 2, 0, h:h + 1]).then_inc(act_step, 1)
                nc.scalar.activation(mprob[:, h % 2, 1, :], v[:, 1, :], ACT.Exp, bias=msm[:, 1, 1, h:h + 1],
                                     scale=MHD ** -0.5, accum_out=msm[:, 2, 1, h:h + 1])\
                    .then_inc(bank_free[BANK[f"ms{h}"]], 1)

            def swa_exp(h):
                act.wait_ge(smax_ready, h + 1)
                s = prob[:, h % 4, :]
                for b, (lo, hi) in enumerate(((0, P), (P, 3 * P))):
                    nc.scalar.activation(s[:, lo:hi], s[:, lo:hi], ACT.Exp, bias=snm[:, b, h:h + 1],
                                         accum_out=sden[:, b, h:h + 1]).then_inc(exp_done, 1)
                nc.scalar.activation(ses[:, :, h:h + 1], snm[:, :, h:h + 1], ACT.Exp,
                                     bias=sink[:, h:h + 1]).then_inc(exp_done, 1)

            def run(names):
                for name in names:
                    if name.startswith("ms"):
                        if int(name[2:]) < 2:
                            mem_exp(int(name[2:]))
                    elif name.startswith("mp"):
                        h = int(name[2:])
                        if h >= 2:
                            wait_full(act, f"mo{h // 2 - 1}")
                        empty(name, mpT[:, h % 2, :, :].rearrange("p a b -> p (a b)"), bank(name))
                        if h + 2 < MH:
                            mem_exp(h + 2)
                    elif name.startswith("mo"):
                        h = int(name[2:])
                        empty(name, y_memT[:, 2 * h:2 * h + 2, :].rearrange("p a b -> p (a b)"), bank(name))
                    elif name.startswith("gate"):
                        n = int(name[4:])
                        wait_full(act, name)
                        for c in range(2):
                            ins = nc.scalar.activation(gate_at[n][:, c, :], bank(name)[:, SEQ * c:SEQ * c + SEQ],
                                                       ACT.Sigmoid, bias=prmT[:, 48 + 2 * n + c:49 + 2 * n + c])
                        ins.then_inc(bank_free[BANK[name]], 1)
                        if name == "gate9":
                            act.wait_ge(y_skip, 1)
                            nc.scalar.activation(y_tm, y_tm, ACT.Gelu_apprx_tanh).then_inc(gelu_done, 1)
                    elif name.startswith("gT"):
                        t = int(name[2:])
                        empty(name, gT[:, :, P * t:P * t + P], bank(name).rearrange("p (k n) -> p k n", k=4))
                    elif name.startswith("gg"):
                        wait_full(act, name)
                        if name == "gg1":
                            wait_emptied(act, "gv0")
                        nc.scalar.activation(sq[:, :], bank(name), ACT.Sigmoid)\
                            .then_inc(bank_free[BANK[name]], 1)
                    elif name.startswith("pv"):
                        j = int(name[2:])
                        empty(name, y_swaT[:, 2 * j:2 * j + 2, :].rearrange("p a b -> p (a b)"), bank(name))
                    elif name.startswith("p"):
                        h = int(name[1:])
                        if h >= 8 and h % 4 == 0:
                            wait_full(act, f"pv{h // 4 - 2}")
                        empty(name, pT[:, h // 4 % 2, h % 4, :, :].rearrange("p a b -> p (a b)"),
                              bank(name)[:, 0:3 * P])
                    elif name.startswith("s"):
                        swa_exp(int(name[1:]))

            act.wait_ge(small_in, 48)
            act.wait_ge(toep_in, 32 * 16)
            run(MEM_STEPS)
            for h in range(2):
                wait_full(act, f"y{h}")
                nc.scalar.copy(y8.rearrange("p t (i h c) -> p i t h c", i=4, h=2)[:, :, :, h, :],
                               bank(f"y{h}").rearrange("p (i t c) -> p i t c", i=4, t=CHUNK))\
                    .then_inc(bank_free[BANK[f"y{h}"]], 1)
            run(SWA_STEPS)
            for t in range(TT):
                act.wait_ge(h2_ready, 1)
                act.wait_ge(sq_done, 4 + t)
                nc.scalar.activation(at(52, D), xres[:, t, :], ACT.Square,
                                     accum_out=ss[:, t:t + 1]).then_inc(sq_done, 1)
            for t in range(TT):
                for h in range(2):
                    empty(f"hT{t}{h}", h2T[:, 4 * h:4 * h + 4, P * t:P * t + P],
                          bank(f"hT{t}{h}").rearrange("p (k n) -> p k n", k=4))
            act.wait_ge(top_ready, 1)
            for t in range(TT):
                ins = nc.scalar.activation(topw[:, t, 0:TOPK], top[:, t, 0:TOPK], ACT.Exp, bias=topw[:, t, 4:5],
                                           accum_out=topw[:, t, 5:6])
                ins.then_inc(topexp_done, 1)
            wait_full(act, "combT")
            nc.scalar.copy(combT[0:EXPERTS, :], bank("combT")[0:EXPERTS, 0:SEQ]).then_inc(bank_free[BANK["combT"]], 1)

            def gather_half(i, n):
                act.wait_ge(gather_full, 2 * i + (n + 1))
                nc.scalar.copy(hgT[:, 4 * n:4 * n + 4, :].rearrange("p k n -> p (k n)"),
                               ps[:, TB, :]).then_inc(gather_ready, 1)

            def act_transposed(e, c):
                act.wait_ge(actT_full, e + (c + 1))
                nc.scalar.copy(actT.rearrange("p a b -> p (a b)"), ps[:, TB, :]).then_inc(actT_ready, 1)

            def sigmoid(e, c):
                act.wait_ge(glu_in, e + (c + 1))
                nc.scalar.activation(hid_s, hid_g, ACT.Sigmoid, scale=ALPHA).then_inc(sig_done, 1)

            def empty_y(e, c):
                act.wait_ge(w2_used, (e + (c + 1)) * KD)
                nc.scalar.copy(y_sb, ps[:, YB, :]).then_inc(y_ready, 1)

            def moe(p):
                gather_half(p * 16, 0)
                gather_half(p * 16, 1)

                def pair(i, first=False, last=False):
                    e = 2 * i
                    if not first:
                        act_transposed(e, -1)
                    sigmoid(e, 0)
                    if not first:
                        empty_y(e, -1)
                    act.wait_ge(scT_full, i + 1)
                    nc.scalar.copy(scT.rearrange("p a b -> p (a b)"), ps[:, TB, :]).then_inc(scT_ready, 1)
                    if not last:
                        gather_half(i + 1, 0)
                    act_transposed(e, 0)
                    sigmoid(e, 1)
                    if not last:
                        gather_half(i + 1, 1)
                    empty_y(e, 0)

                pair(p * 16, first=True)
                with act.Fori(1, 15) as i:
                    pair(i + p * 16)
                pair(p * 16 + 15, last=True)
                act_transposed(p * EXPERTS, EXPERTS - 1)
                empty_y(p * EXPERTS, EXPERTS - 1)

            moe(0)
            act.wait_ge(count_ready, 1)
            most = act.value_load(count[0:1, 0:1], min_val=0, max_val=SEQ)
            with act.Fori(1, PASSES) as p:
                with act.If(most > p * SLOTS):
                    moe(p)

        @block.tensor
        def _(pe):
            mm = nc.tensor.matmul

            def begin(name):
                if TURN[name] > 1:
                    pe.wait_ge(bank_free[BANK[name]], TURN[name] - 1)
                return bank(name)

            def end(ins, name):
                ins.then_inc(bank_full[BANK[name]], 1)

            def transposes(name, tiles):
                o, col = begin(name), 0
                for t in tiles:
                    n = t.shape[0]
                    ins = nc.tensor.transpose(o[0:t.free_size(), col:col + n], t, ident[0:n, 0:n])
                    col += n
                end(ins, name)

            def wait_block(name):
                pe.wait_ge(loaded[SLOT_OF[name]], 16 * LOADS_OF[name] + (16 if name == "glu" else 0)
                           + (16 if SLOT_OF[name] == SLOT_OF["glu"] and BLOCKS.index(name) > BLOCKS.index("glu") else 0))
                return ring[:, SLOT_OF[name], :]

            def token_major(name, blk, lhs, t):
                w = wait_block(blk).rearrange("p (k n) -> p k n", k=KD)
                o = begin(name)
                for k in range(KD):
                    ins = mm(o, lhs[:, k, P * t:P * t + P], w[:, k, :], start=(k == 0), stop=(k == KD - 1))
                end(ins, name)

            pe.wait_ge(consts, 1)
            pe.wait_ge(prm_in, 5 * 16)
            pe.wait_ge(ldt_ready, 1)
            transposes("param", [prm[:, :]])
            for t in range(TT):
                pe.wait_ge(h_ready, t + 1)
                for h in range(2):
                    transposes(f"xT{t}{h}", [h_tm[:, t, P * k:P * k + P] for k in range(4 * h, 4 * h + 4)])
            for t in range(TT):
                for h in range(2):
                    wait_emptied(pe, f"xT{t}{h}")
            for t in range(TT):
                token_major(f"u{t}", "u", hT, t)
            pe.wait_ge(cr_in, 8 * 16)
            transposes("cparam", [c_raw[:, i, r, :] for i in range(2) for r in range(2)])
            for n in range(2):
                for t in range(TT):
                    token_major(f"q{n}{t}", f"q{n}", hT, t)
            for t in range(TT):
                token_major(f"kv{t}", "kv", hT, t)
            for t in range(TT):
                pe.wait_ge(mem_ready, t + 1)
                for h in range(2):
                    transposes(f"memT{t}{h}", [mem_tm[:, t, P * k:P * k + P] for k in range(4 * h, 4 * h + 4)])
            for t in range(TT):
                for h in range(2):
                    wait_emptied(pe, f"memT{t}{h}")
            for t in range(TT):
                token_major(f"mk{t}", "mk", memT, t)
            for t in range(TT):
                token_major(f"mv{t}", "mv", memT, t)
            for t in range(TT):
                token_major(f"qm{t}", "qm", hT, t)

            pe.wait_ge(ab_ready, 1)
            pe.wait_ge(ca_ready, 1)
            o = [begin(f"lag{h}") for h in range(2)]
            for r in range(4):
                for i, (ab, ca) in enumerate(((ab_re, ca_re), (ab_im, ca_im))):
                    for j in range(4):
                        for h in range(2):
                            s, q = slice(STATE * h, STATE * h + STATE), 4 * r + j
                            ins = mm(o[h][32 * j:32 * j + GCH, P * r:P * r + P], ab[s, q, CHUNK - 1, :],
                                     ca[s, q, 0:CHUNK, :], start=(i == 0), stop=(i == 1), skip_group_check=True)
                            if (r, i, j) == (3, 1, 3):
                                end(ins, f"lag{h}")
            for n in range(8):
                transposes(f"in{n}", [v[:, 2 * n + q, :, :].rearrange("p t c -> p (t c)")
                                      for q in range(2) for v in (ab_re, ab_im)])
            pe.wait_ge(u8g_ready, 1)
            for n in range(2):
                transposes(f"uT{n}", [u8g[:, i, :, :].rearrange("p t c -> p (t c)") for i in range(4 * n, 4 * n + 4)])
            for n in range(8):
                wait_emptied(pe, f"in{n}")
            for n in range(2):
                wait_emptied(pe, f"uT{n}")
            for name, w in (("xre", win_re), ("xim", win_im)):
                o = begin(name)
                for q in range(PAIRS):
                    for h in range(2):
                        ins = mm(o[STATE * h:STATE * h + STATE, NCHUNK * q:NCHUNK * q + NCHUNK],
                                 w[:, q, STATE * h:STATE * h + STATE], uT[:, (2 * q + h) % 8, (2 * q + h) // 8, :],
                                 start=True, stop=True, skip_group_check=True)
                end(ins, name)
            pe.wait_ge(qk_ready, 4)
            for t in range(TT):
                for h in range(2):
                    transposes(f"qT{t}{h}", [q_tm[:, t, P * k:P * k + P] for k in range(4 * h, 4 * h + 4)])
            pe.wait_ge(qk_ready, 6)
            for t in range(TT):
                transposes(f"kT{t}", [kdup[:, t, j, :, :].rearrange("p a b -> p (a b)") for j in range(KVH)])
            pe.wait_ge(qk_ready, 8)
            for t in range(TT):
                transposes(f"mkT{t}", [mk_tm[:, t, P * h:P * h + P] for h in range(MH)])
            pe.wait_ge(qk_ready, 10)
            for t in range(TT):
                transposes(f"qmT{t}", [qm_tm[:, t, P * h:P * h + P] for h in range(MH)])
            def mem_scores(h):
                o = begin(f"ms{h}")
                for t in range(TT):
                    ins = mm(o[:, SEQ * t:SEQ * t + SEQ], qmT[:, h, P * t:P * t + P], mkT[:, h, :],
                             start=True, stop=True, skip_group_check=True)
                end(ins, f"ms{h}")

            def scores(h):
                for cols, rows in (((0, P), (0, P)), ((P, 3 * P), (P, SEQ))):
                    for i in (h, h + 1):
                        o = begin(f"s{i}") if cols[0] == 0 else bank(f"s{i}")
                        s = slice(HD * (i % 2), HD * (i % 2) + HD)
                        ins = mm(o[:, cols[0]:cols[1]], qT[s, i // 2, rows[0]:rows[1]],
                                 kT[s, i // 4, 0:cols[1] - cols[0]], start=True, stop=True,
                                 skip_group_check=True)
                        if cols[0]:
                            end(ins, f"s{i}")

            def chunk_outputs():
                o = [begin(f"y{h}") for h in range(2)]
                for i in range(4):
                    for h in range(2):
                        for r in range(4):
                            mm(o[h][32 * r:32 * r + NCHUNK, P * i:P * i + P], uT[:, 2 * i + h, r, :],
                               toep[:, i, h, r, :], start=(i == 0), stop=False, skip_group_check=True)
                for i in range(4):
                    for part, ca in enumerate((ca_re, ca_im)):
                        for r in range(4):
                            for h in range(2):
                                s, q = slice(STATE * h, STATE * h + STATE), 4 * r + i
                                ins = mm(o[h][32 * r:32 * r + NCHUNK, P * i:P * i + P], st[s, part, q, :],
                                         ca[s, q, 1:CHUNK + 1, :], start=False,
                                         stop=(i == 3 and part == 1), skip_group_check=True)
                                if (i, part, r) == (3, 1, 3):
                                    end(ins, f"y{h}")

            def weighted_values(j):
                o = begin(f"pv{j}").rearrange("p (a n) -> p a n", a=2)
                for qb, blk, kb, st_, sp_ in ((0, 0, 0, True, True), (1, 1, 0, True, False), (1, 2, 1, False, True)):
                    for par in range(2):
                        ins = mm(o[HD * par:HD * par + HD, :, P * qb:P * qb + P],
                                 kv_tm[:, kb, 256 + HD * j:256 + HD * j + HD], pT[:, j % 2, par::2, blk, :],
                                 start=st_, stop=sp_, skip_group_check=True)
                end(ins, f"pv{j}")

            def channel_major(name, w, rhs, chans, kn):
                o = begin(name)
                for c, ch in enumerate(chans):
                    for k in range(kn):
                        ins = mm(o[:, SEQ * c:SEQ * c + SEQ], w[:, k, P * ch:P * ch + P], rhs[:, k, :],
                                 start=(k == 0), stop=(k == kn - 1), skip_group_check=True)
                end(ins, name)

            def run(names):
                for name in names:
                    if name.startswith("mp"):
                        h = int(name[2:])
                        pe.wait_ge(mprob_ready, h + 1)
                        transposes(name, [mprob[:, h % 2, t, P * kb:P * kb + P]
                                          for kb in range(2) for t in range(TT)])
                    elif name.startswith("ms"):
                        mem_scores(int(name[2:]))
                    elif name.startswith("mo"):
                        g = int(name[2:])
                        o = begin(name)
                        for h in (2 * g, 2 * g + 1):
                            wait_emptied(pe, f"mp{h}")
                            for kb in range(2):
                                ins = mm(o[:, SEQ * (h % 2):SEQ * (h % 2) + SEQ], mv_tm[:, kb, P * h:P * h + P],
                                         mpT[:, h % 2, kb, :], start=(kb == 0), stop=(kb == 1),
                                         skip_group_check=True)
                        end(ins, name)
                    elif name.startswith("gate"):
                        n = int(name[4:])
                        w = wait_block(f"gate{n // 2}").rearrange("p (k n) -> p k n", k=KD)
                        channel_major(name, w, hT, (2 * (n % 2), 2 * (n % 2) + 1), KD)
                    elif name.startswith("gT"):
                        t = int(name[2:])
                        pe.wait_ge(gelu_done, 1)
                        transposes(name, [y_tm[:, t, P * k:P * k + P] for k in range(4)])
                    elif name.startswith("gv") or name.startswith("gg"):
                        i, n = ("gv", "gg").index(name[:2]), int(name[2:])
                        for t in range(TT):
                            wait_emptied(pe, f"gT{t}")
                        w = wait_block("glu")[:, 2048 * i:2048 * i + 2048].rearrange("p (k n) -> p k n", k=4)
                        channel_major(name, w, gT, (2 * n, 2 * n + 1), 4)
                    elif name.startswith("pv"):
                        j = int(name[2:])
                        for h in range(4 * j, 4 * j + 4):
                            wait_emptied(pe, f"p{h}")
                        weighted_values(j)
                    elif name.startswith("p"):
                        h = int(name[1:])
                        pe.wait_ge(prob_ready, h + 1)
                        transposes(name, [prob[:, h % 4, P * b:P * b + P] for b in range(3)])
                    elif int(name[1:]) % 2 == 0:
                        scores(int(name[1:]))

            for n in ("qmT", "mkT"):
                for t in range(TT):
                    wait_emptied(pe, f"{n}{t}")
            run(MEM_STEPS)
            pe.wait_ge(scan_done, 1)
            pe.wait_ge(toep_in, 32 * 16)
            chunk_outputs()
            for t in range(TT):
                for h in range(2):
                    wait_emptied(pe, f"qT{t}{h}")
                wait_emptied(pe, f"kT{t}")
            run(SWA_STEPS)
            for j in range(4):
                wait_emptied(pe, f"pv{j}")
            for i in range(4):
                w = wait_block(f"swa{i // 2}").rearrange("p (k n) -> p k n", k=KD)
                channel_major(f"br1{i}", w, y_swaT, (2 * (i % 2), 2 * (i % 2) + 1), KD)
            for n in range(2):
                wait_emptied(pe, f"gv{n}")
            for i in range(4):
                w = wait_block("ssm").rearrange("p (k n) -> p k n", k=4)
                channel_major(f"br0{i}", w, y_ssmT, (2 * i, 2 * i + 1), 4)
            for j in range(2):
                wait_emptied(pe, f"mo{j}")
            for i in range(4):
                w = wait_block("mem").rearrange("p (k n) -> p k n", k=4)
                channel_major(f"br2{i}", w, y_memT, (2 * i, 2 * i + 1), 4)
            pe.wait_ge(merged_ready, 4)
            for n in range(2):
                for t in range(TT):
                    w = wait_block(f"out{n}").rearrange("p (k n) -> p k n", k=KD)
                    o = begin(f"o{t}{n}")
                    for k in range(KD):
                        ins = mm(o, merged[:, k, P * t:P * t + P], w[:, k, :], start=(k == 0), stop=(k == KD - 1))
                    end(ins, f"o{t}{n}")
            for t in range(TT):
                pe.wait_ge(h2_ready, 2 + t)
                for h in range(2):
                    transposes(f"hT{t}{h}", [h2[:, t, P * k:P * k + P] for k in range(4 * h, 4 * h + 4)])
            for t in range(TT):
                for h in range(2):
                    wait_emptied(pe, f"hT{t}{h}")
            pe.wait_ge(router_in, 32)
            o = begin("logit")
            for t in range(TT):
                for k in range(KD):
                    ins = mm(o[:, EXPERTS * t:EXPERTS * t + EXPERTS], h2T[:, k, P * t:P * t + P], wr_sb[:, k, :],
                             start=(k == 0), stop=(k == KD - 1), skip_group_check=True)
            end(ins, "logit")
            pe.wait_ge(chosen_ready, 1)
            pe.wait_ge(consts, 3)
            o = begin("pos")
            mm(o[:, 0:32], before_bf[:, :], chosen[:, 0, :], start=True, stop=True, skip_group_check=True)
            mm(o[:, 32:64], before_bf[:, :], chosen[:, 1, :], start=True, stop=False, skip_group_check=True)
            mm(o[:, 32:64], ones_bf[:, :], chosen[:, 0, :], start=False, stop=True, skip_group_check=True)
            mm(o[:, 64:96], ones_bf[:, :], chosen[:, 0, :], start=True, stop=False, skip_group_check=True)
            end(mm(o[:, 64:96], ones_bf[:, :], chosen[:, 1, :], start=False, stop=True, skip_group_check=True), "pos")
            transposes("combT", [comb[:, t, :] for t in range(TT)])
            pe.wait_ge(late_in, 32)
            wait_emptied(pe, "combT")
            for b in range(8):
                pe.wait_ge(bank_free[b], TURNS[b])
            for t in range(TT):
                for n in range(2):
                    ins = mm(acc[t][n], combT[0:EXPERTS, P * t:P * t + P], b2_sb[0:EXPERTS, 512 * n:512 * n + 512],
                             start=True, stop=False, skip_group_check=True)

            def gather(i, n):
                for k in range(4):
                    for t in range(TT):
                        ins = mm(ps[:, TB, P * k:P * k + P], h2[:, t, P * (4 * n + k):P * (4 * n + k) + P],
                                 onehot[:, t, :], start=(t == 0), stop=(t == TT - 1), skip_group_check=True)
                ins.then_inc(gather_full, 1)

            def first_matrix(eg, par, wait_hid):
                if wait_hid:
                    pe.wait_ge(hid_free, eg + (par if par else 0))
                pe.wait_ge(row_ready, eg + (par + 1))
                for n in range(2):
                    for h in range(2):
                        q = 2 * n + h
                        mm(ps[SLOTS * h:SLOTS * h + SLOTS, H0 + n, :], bias_row[:, par, :],
                           b1_sb[:, 512 * q:512 * q + 512], start=True, stop=False, skip_group_check=True)
                for k in range(KD):
                    pe.wait_ge(w1_loaded[k], (eg + (par + 1)) * 16)
                    w = ring[:, k // 2, (k % 2) * 2048:(k % 2) * 2048 + 2048]
                    for n in range(2):
                        for h in range(2):
                            q = 2 * n + h
                            ins = mm(ps[SLOTS * h:SLOTS * h + SLOTS, H0 + n, :],
                                     hgT[:, k, SLOTS * par:SLOTS * par + SLOTS], w[:, 512 * q:512 * q + 512],
                                     start=False, stop=(k == KD - 1), skip_group_check=True)
                    ins.then_inc(w1_used, 1)

            def act_transposes(eg, par, c):
                pe.wait_ge(act_ready, eg + (c + 1))
                for n in range(2):
                    for j in range(2):
                        ins = nc.tensor.transpose(ps[:, TB, P * (2 * n + j):P * (2 * n + j) + P],
                                                  act_sb[:, par, n, P * j:P * j + P], ident[:, :])
                ins.then_inc(actT_full, 1)

            def second_matrix(eg, c):
                pe.wait_ge(actT_ready, eg + (c + 1))
                for r in range(KD):
                    n, h, j = r // 4, r // 2 % 2, r % 2
                    pe.wait_ge(w2_loaded[r], (eg + (c + 1)) * 16)
                    for o in range(2):
                        ins = mm(ps[SLOTS * o:SLOTS * o + SLOTS, YB, :],
                                 actT[:, 2 * n + j, SLOTS * h:SLOTS * h + SLOTS],
                                 w2ring[:, r * D + 512 * o:r * D + 512 * o + 512],
                                 start=(r == 0), stop=(r == KD - 1), skip_group_check=True)
                    ins.then_inc(w2_used, 1)

            def scatter(eg, par, c):
                pe.wait_ge(y_ready, eg + (c + 1))
                for t in range(TT):
                    for h in range(2):
                        ins = mm(acc[t][h], scT[SLOTS * h:SLOTS * h + SLOTS, par, P * t:P * t + P],
                                 y_sb[SLOTS * h:SLOTS * h + SLOTS, :], start=False, stop=False,
                                 skip_group_check=True)
                ins.then_inc(scattered, 1)

            def moe(p, first_pass):
                eg0 = p * EXPERTS
                pe.wait_ge(onehot_ready, p * 16 + 1)
                if not first_pass:
                    pe.wait_ge(actT_ready, eg0)
                gather(p * 16, 0)
                pe.wait_ge(gather_ready, (p * 16) * 2 + 1)
                gather(p * 16, 1)
                pe.wait_ge(gather_ready, (p * 16) * 2 + 2)

                def pair(i, first=False, last=False):
                    e = 2 * i
                    pe.wait_ge(gather_ready, i * 2 + 2)
                    first_matrix(e, 0, not (first and first_pass))
                    if not first:
                        scatter(e, 0, -2)
                        act_transposes(e, 1, -1)
                        second_matrix(e, -1)
                    first_matrix(e, 1, True)
                    if not first:
                        scatter(e, 1, -1)
                    pe.wait_ge(weighted_ready, i + 1)
                    if not first:
                        pe.wait_ge(actT_ready, e)
                    for a in range(2):
                        for t in range(TT):
                            ins = nc.tensor.transpose(ps[:, TB, SEQ * a + P * t:SEQ * a + P * t + P],
                                                      onehot_w[:, a, t, :], ident[:, :])
                    ins.then_inc(scT_full, 1)
                    pe.wait_ge(scT_ready, i + 1)
                    if not last:
                        pe.wait_ge(onehot_ready, i + 2)
                        gather(i + 1, 0)
                        pe.wait_ge(gather_ready, i * 2 + 3)
                    act_transposes(e, 0, 0)
                    pe.wait_ge(actT_ready, e + 1)
                    if not last:
                        gather(i + 1, 1)
                    second_matrix(e, 0)

                pair(p * 16, first=True)
                with pe.Fori(1, 15) as i:
                    pair(i + p * 16)
                pair(p * 16 + 15, last=True)
                scatter(eg0, 0, EXPERTS - 2)
                act_transposes(eg0, 1, EXPERTS - 1)
                second_matrix(eg0, EXPERTS - 1)
                scatter(eg0, 1, EXPERTS - 1)

            moe(0, True)
            pe.wait_ge(count_ready, 1)
            most = pe.value_load(count[0:1, 0:1], min_val=0, max_val=SEQ)
            with pe.Fori(1, PASSES) as p:
                with pe.If(most > p * SLOTS):
                    moe(p, False)
            pe.drain().then_inc(acc_full, 1)

        @block.vector
        def _(dve):
            steps = [0]
            V = nc.vector

            def link(ins, s=None, n=None):
                if s is None:
                    steps[0] += 1
                    s, n = dve_step, steps[0]
                ins.then_inc(s, 1)
                dve.wait_ge(s, n)

            def free(ins, name):
                link(ins, bank_free[BANK[name]], TURN[name])

            dve.wait_ge(ldt_in, 16)
            V.tensor_copy(prm[32:48, :].rearrange("q (h s) -> q h s", h=2),
                          ldt_raw[32:48, :].unsqueeze(2).broadcast_to([PAIRS, 2, STATE])).then_inc(ldt_ready, 1)
            def token_norm(i, src, dst, g, arrived, ready):
                dve.wait_ge(rstd_done, i + 1)
                dve.wait_ge(arrived, 16)
                for t in range(TT):
                    V.scalar_tensor_tensor(dst[:, t, :], src[:, t, :], ss[:, 2 * i + t:2 * i + t + 1], g,
                                           op0=ALU.mult, op1=ALU.mult).then_inc(ready, 1)

            token_norm(0, xres, h_tm, g_attn, gx_in, h_ready)

            T = [tb[:, i, :] for i in range(26)]

            def tt(o, a, b, op):
                link(V.tensor_tensor(o, a, b, op))

            def tsc(o, a, s1, op0, s2=None, op1=None):
                if s2 is None:
                    link(V.tensor_scalar(o, a, s1, None, op0))
                else:
                    link(V.tensor_scalar(o, a, s1, s2, op0, op1))

            def stt(o, a, s, b, op0, op1):
                link(V.scalar_tensor_tensor(o, a, s, b, op0=op0, op1=op1))

            def reduce_angle(r, x, q):
                tsc(q, x, 1.0 / (2 * np.pi), ALU.mult, MAGIC, ALU.add)
                tsc(q, q, MAGIC, ALU.subtract)
                stt(r, q, -TWO_PI[0], x, ALU.mult, ALU.add)
                stt(r, q, -TWO_PI[1], r, ALU.mult, ALU.add)
                stt(r, q, -TWO_PI[2], r, ALU.mult, ALU.add)
                tsc(r, r, PI_BOUND, ALU.min, -PI_BOUND, ALU.max)

            wait_emptied(dve, "param")
            a_re, a_im, ldt = prmT[:, 0:16], prmT[:, 16:32], prmT[:, 32:48]
            x_, q_, r_, p_, dt_ = T[0], T[1], T[2], T[3], T[4]
            tsc(x_, ldt, 88.0, ALU.min, -87.0, ALU.max)
            tsc(q_, x_, float(1 / np.log(2)), ALU.mult, MAGIC, ALU.add)
            tsc(q_, q_, MAGIC, ALU.subtract)
            stt(r_, q_, -LN2[0], x_, ALU.mult, ALU.add)
            stt(r_, q_, -LN2[1], r_, ALU.mult, ALU.add)
            tsc(p_, r_, 1 / 5040., ALU.mult)
            for c in (1 / 720., 1 / 120., 1 / 24., 1 / 6., 0.5, 1.0):
                stt(p_, p_, c, r_, ALU.add, ALU.mult)
            tsc(p_, p_, 1.0, ALU.add)
            link(V.tensor_scalar(tbi[:, :], q_, 127.0, 2.0 ** 23, ALU.add, ALU.mult))
            tt(dt_, p_, tbi[:, :].bitcast(F32), ALU.mult)
            re_, im_, th = T[5], a_im, T[6]
            tsc(re_, a_re, -1e-4, ALU.min)
            tt(th, im_, dt_, ALU.mult)
            reduce_angle(T[8], th, q_)
            tsc(T[9], T[8], 0.5, ALU.mult)
            link(V.tensor_copy(q_, T[9]), angle_ready, 1)
            dve.wait_ge(posi_in, 32)
            dve.wait_ge(consts, 6)
            link(V.tensor_copy(posf[:, :], posi[:, :]))
            for t in range(TT):
                tsc(rope[:, 4, t, :], freq[:, :], posf[:, t:t + 1], ALU.mult)
            flat = [rope[:, i, :, :].rearrange("p t f -> p (t f)") for i in range(6)]
            reduce_angle(flat[0], flat[4], flat[5])
            link(V.tensor_scalar(flat[1], flat[0], 0.5, None, ALU.mult), angle_ready, 2)
            token_norm(1, mem_tm, mem_tm, g_mem, gm_in, mem_ready)
            E = T[7]
            tt(x_, re_, dt_, ALU.mult)
            tsc(x_, x_, -88.0, ALU.max, 1 / 128., ALU.mult)
            tsc(E, x_, 1 / 5040., ALU.mult)
            for c in (1 / 720., 1 / 120., 1 / 24., 1 / 6., 0.5, 1.0):
                stt(E, E, c, x_, ALU.add, ALU.mult)
            for _ in range(7):
                stt(E, E, 2.0, E, ALU.add, ALU.mult)
            dve.wait_ge(sin_done, 1)
            sn, hf = T[10], T[11]
            cos_, am_re, am_im = T[12], T[13], T[14]
            tt(q_, hf, hf, ALU.mult)
            tsc(cos_, q_, -2.0, ALU.mult, 1.0, ALU.add)
            tt(am_re, E, cos_, ALU.mult)
            stt(am_re, q_, -2.0, am_re, ALU.mult, ALU.add)
            stt(am_im, E, 1.0, sn, ALU.add, ALU.mult)
            link(V.memset(pw_re[:, 0, :], 1.0))
            link(V.memset(pw_im[:, 0, :], 0.0))
            stt(pw_re[:, 1, :], E, 1.0, cos_, ALU.add, ALU.mult)
            link(V.tensor_copy(pw_im[:, 1, :], am_im))
            t0, t1 = T[16:20], T[20:24]
            for n in (1, 2, 4):
                s0, s1 = tb[:, 16:16 + n, :], tb[:, 20:20 + n, :]
                lo = slice(1, 1 + n)
                hi = slice(1 + n, 1 + 2 * n)
                br = pw_re[:, n, :].unsqueeze(1).broadcast_to([P, n, PAIRS])
                bi = pw_im[:, n, :].unsqueeze(1).broadcast_to([P, n, PAIRS])
                tt(s0, pw_re[:, lo, :], br, ALU.mult)
                tt(s1, pw_im[:, lo, :], bi, ALU.mult)
                tt(pw_re[:, hi, :], s0, s1, ALU.subtract)
                tt(s0, pw_re[:, lo, :], bi, ALU.mult)
                tt(s1, pw_im[:, lo, :], br, ALU.mult)
                tt(pw_im[:, hi, :], s0, s1, ALU.add)
            d_, f_re, f_im = T[15], T[16], T[17]
            tt(T[18], re_, re_, ALU.mult)
            tt(T[19], im_, im_, ALU.mult)
            tt(d_, T[18], T[19], ALU.add)
            link(V.reciprocal(d_, d_))
            tt(T[18], am_re, re_, ALU.mult)
            tt(T[19], am_im, im_, ALU.mult)
            tt(T[18], T[18], T[19], ALU.add)
            tt(f_re, T[18], d_, ALU.mult)
            tt(T[18], am_im, re_, ALU.mult)
            tt(T[19], am_re, im_, ALU.mult)
            tt(T[18], T[18], T[19], ALU.subtract)
            tt(f_im, T[18], d_, ALU.mult)
            dve.wait_ge(bc_in, 64)
            fr = f_re.unsqueeze(2).broadcast_to([P, PAIRS, GCH])
            fi = f_im.unsqueeze(2).broadcast_to([P, PAIRS, GCH])
            tmp = sq[:, 0:256].rearrange("p (q c) -> p q c", q=PAIRS)
            tt(bb_re, b_re, fr, ALU.mult)
            tt(tmp, b_im, fi, ALU.mult)
            tt(bb_re, bb_re, tmp, ALU.subtract)
            tt(bb_im, b_im, fr, ALU.mult)
            tt(tmp, b_re, fi, ALU.mult)
            link(V.tensor_tensor(bb_im, bb_im, tmp, ALU.add), powers_ready, 1)
            for i in range(2):
                link(V.tensor_copy(a8[:, 0, i, :], pw_re[:, CHUNK, :]))
            tsc(a8[:, 1, 0, :], pw_im[:, CHUNK, :], -1.0, ALU.mult)
            link(V.tensor_copy(a8[:, 1, 1, :], pw_im[:, CHUNK, :]))
            wait_emptied(dve, "cparam")
            full = [P, PAIRS, CHUNK + 1, GCH]
            cr, ci = (v.unsqueeze(2).broadcast_to(full) for v in (c_re, c_im))
            pr, pi = (v[:, :, :].rearrange("p t q -> p q t").unsqueeze(3).broadcast_to(full) for v in (pw_re, pw_im))
            tt(ca_re, cr, pr, ALU.mult)
            tt(ca_tmp, ci, pi, ALU.mult)
            tt(ca_re, ca_re, ca_tmp, ALU.subtract)
            tt(ca_im, cr, pi, ALU.mult)
            tt(ca_tmp, ci, pr, ALU.mult)
            tt(ca_im, ca_im, ca_tmp, ALU.add)
            link(V.tensor_scalar(ca_im, ca_im, -1.0, None, ALU.mult), ca_ready, 1)

            dve.wait_ge(sin_done, 2)
            tt(flat[5], flat[3], flat[3], ALU.mult)
            tsc(flat[3], flat[5], -2.0, ALU.mult, 1.0, ALU.add)

            asked = [0]

            def sums(v, heads, width):
                i = asked[0]
                s = sq[:, 0:heads * width].rearrange("p (h d) -> p h d", h=heads)
                tt(s, v, v, ALU.mult)
                asked[0] += 1
                link(V.tensor_reduce(hs[:, i, 0:heads], s, AX.X, ALU.add), rstd_asked, i + 1)
                return hs[:, i, 0:heads]

            def normed(v, r, i, heads, width):
                dve.wait_ge(rstd_done, 2 + i + 1)
                return V.tensor_tensor(v, v, r.unsqueeze(2).broadcast_to([P, heads, width]), ALU.mult)

            def rotate(v, t, heads, dst):
                sh = [P, heads, ROPE_HALF]
                a = [rtmp[:, i, 0:heads * ROPE_HALF].rearrange("p (h f) -> p h f", h=heads) for i in range(4)]
                s = rope[:, 2, t, :].unsqueeze(1).broadcast_to(sh)
                c = rope[:, 3, t, :].unsqueeze(1).broadcast_to(sh)
                t1, t2 = v[:, :, 0:ROPE_HALF], v[:, :, ROPE_HALF:2 * ROPE_HALF]
                tt(a[0], t1, c, ALU.mult)
                tt(a[1], t2, s, ALU.mult)
                tt(a[2], t2, c, ALU.mult)
                tt(a[3], t1, s, ALU.mult)
                tt(dst[:, :, 0:ROPE_HALF], a[0], a[1], ALU.subtract)
                return V.tensor_tensor(dst[:, :, ROPE_HALF:2 * ROPE_HALF], a[2], a[3], ALU.add)

            dve.wait_ge(small_in, 48)
            for n in range(2):
                for t in range(TT):
                    wait_emptied(dve, f"q{n}{t}")
            heads8 = [(t, q_tm[:, t, 512 * n:512 * n + 512].rearrange("p (h d) -> p h d", h=8))
                      for n in range(2) for t in range(TT)]
            r_of = [sums(v, 8, HD) for _, v in heads8]
            for t in range(TT):
                wait_emptied(dve, f"kv{t}")
            keys = [kv_tm[:, t, 0:256].rearrange("p (h d) -> p h d", h=KVH) for t in range(TT)]
            r_of += [sums(v, KVH, HD) for v in keys]
            for i, (t, v) in enumerate(heads8):
                link(normed(v, r_of[i], i, 8, HD))
                tt(v, v, gain_q[:, :].unsqueeze(1).broadcast_to([P, 8, HD]), ALU.mult)
                link(rotate(v, t, 8, v), qk_ready, i + 1)
            for t, v in enumerate(keys):
                link(normed(v, r_of[4 + t], 4 + t, KVH, HD))
                tt(v, v, gain_k[:, :].unsqueeze(1).broadcast_to([P, KVH, HD]), ALU.mult)
                link(rotate(v, t, KVH, v))
                link(V.tensor_copy(kdup[:, t, :, 0, :], v))
                link(V.tensor_copy(kdup[:, t, :, 1, :], v), qk_ready, 5 + t)
            for i, (name, tm) in enumerate((("mk", mk_tm), ("qm", qm_tm))):
                for t in range(TT):
                    wait_emptied(dve, f"{name}{t}")
                v = [tm[:, t, :].rearrange("p (h d) -> p h d", h=MH) for t in range(TT)]
                r_of = [sums(v[t], MH, MHD) for t in range(TT)]
                for t in range(TT):
                    link(normed(v[t], r_of[t], 6 + 2 * i + t, MH, MHD), qk_ready, 7 + 2 * i + t)

            def mem_max(h):
                wait_full(dve, f"ms{h}")
                v = bank(f"ms{h}").rearrange("p (t n) -> p t n", t=TT)
                link(V.tensor_reduce(msm[:, 0, :, h], v, AX.X, ALU.max))
                V.tensor_scalar(msm[:, 1, :, h], msm[:, 0, :, h], -MHD ** -0.5, None, ALU.mult)\
                    .then_inc(mmax_ready, 1)

            def mem_scale(h):
                wait_emptied(dve, f"ms{h}")
                link(V.reciprocal(msm[:, 3, :, h], msm[:, 2, :, h]))
                for t in range(TT):
                    ins = V.tensor_scalar(mprob[:, h % 2, t, :], mprob[:, h % 2, t, :], msm[:, 3, t, h:h + 1],
                                          None, ALU.mult)
                    if t == 0:
                        link(ins)
                ins.then_inc(mprob_ready, 1)

            def swa_max(h):
                wait_full(dve, f"s{h}")
                if h >= 4:
                    wait_full(dve, f"p{h - 4}")
                s = prob[:, h % 4, :]
                free(V.scalar_tensor_tensor(s, bank(f"s{h}")[:, 0:3 * P], HD ** -0.5, mask[:, :],
                                            op0=ALU.mult, op1=ALU.add), f"s{h}")
                link(V.tensor_reduce(smx[:, 0, h:h + 1], s[:, 0:P], AX.X, ALU.max))
                link(V.tensor_reduce(smx[:, 1, h:h + 1], s[:, P:3 * P], AX.X, ALU.max))
                V.tensor_scalar(snm[:, :, h], smx[:, :, h], sink[:, h:h + 1], -1.0, ALU.max, ALU.mult)\
                    .then_inc(smax_ready, 1)

            def swa_scale(h):
                dve.wait_ge(exp_done, 3 * h + 3)
                s = prob[:, h % 4, :]
                tt(sden[:, :, h], sden[:, :, h], ses[:, :, h], ALU.add)
                link(V.reciprocal(sden[:, :, h], sden[:, :, h]))
                link(V.tensor_scalar(s[:, 0:P], s[:, 0:P], sden[:, 0, h:h + 1], None, ALU.mult))
                V.tensor_scalar(s[:, P:3 * P], s[:, P:3 * P], sden[:, 1, h:h + 1], None, ALU.mult)\
                    .then_inc(prob_ready, 1)

            def skip():
                dve.wait_ge(d_in, 16)
                dve.wait_ge(y8_out, 8 * 16)
                for t in range(TT):
                    tt(sq[:, :], u_tm[:, t, :], d_bc[:, :], ALU.mult)
                    ins = V.tensor_tensor(y_tm[:, t, :], y_tm[:, t, :], sq[:, :], ALU.add)
                    if t == 0:
                        link(ins)
                link(ins, y_skip, 1)

            dve.wait_ge(consts, 2)
            for h in range(MH):
                mem_max(h)
            for h in range(MH):
                mem_scale(h)
            for h in range(2):
                wait_full(dve, f"y{h}")
            swa_max(0)
            swa_max(1)
            for h in range(2, HEADS + 2, 2):
                if h < HEADS:
                    swa_max(h)
                    swa_max(h + 1)
                swa_scale(h - 2)
                swa_scale(h - 1)
                if h == 4:
                    skip()
            for n in range(2):
                wait_full(dve, f"gv{n}")
                wait_emptied(dve, f"gg{n}")
                ins = V.tensor_tensor(y_ssmT[:, 2 * n:2 * n + 2, :].rearrange("p a b -> p (a b)"),
                                      bank(f"gv{n}"), sq[:, :], ALU.mult)
                free(ins, f"gv{n}")

            for b in (1, 0, 2):
                for i in range(4):
                    wait_full(dve, f"br{b}{i}")
                    if b == 1 and i == 0:
                        for g in range(12):
                            wait_emptied(dve, f"gate{g}")
                        wait_full(dve, "mo1")
                    g = gate_at[4 * b + i].rearrange("p a b -> p (a b)")
                    m = merged[:, 2 * i:2 * i + 2, :].rearrange("p a b -> p (a b)")
                    if b == 1:
                        free(V.tensor_tensor(m, bank(f"br{b}{i}"), g, ALU.mult), f"br{b}{i}")
                        continue
                    free(V.tensor_tensor(sq[:, :], bank(f"br{b}{i}"), g, ALU.mult), f"br{b}{i}")
                    if b == 2:
                        link(V.tensor_tensor(m, m, sq[:, :], ALU.add), merged_ready, i + 1)
                    else:
                        tt(m, m, sq[:, :], ALU.add)
            for t in range(TT):
                for n in range(2):
                    wait_full(dve, f"o{t}{n}")
                    v = xres[:, t, 512 * n:512 * n + 512]
                    free(V.tensor_tensor(v, bank(f"o{t}{n}"), v, ALU.add), f"o{t}{n}")
            link(V.tensor_copy(cmax[:, :], xres[:, 0, 0:1]), h2_ready, 1)
            dve.wait_ge(rstd_done, 13)
            dve.wait_ge(gf_in, 16)
            for t in range(TT):
                link(V.scalar_tensor_tensor(h2[:, t, :], xres[:, t, :], ss[:, t:t + 1], g_ffn,
                                            op0=ALU.mult, op1=ALU.mult), h2_ready, 2 + t)
            wait_full(dve, "logit")
            dve.wait_ge(router_in, 32)
            o = bank("logit")[:, 0:2 * EXPERTS].rearrange("p (t e) -> p t e", t=TT)
            free(V.tensor_tensor(lg[:, :, :], o, br_bc[:, :].unsqueeze(1).broadcast_to([P, TT, EXPERTS]),
                                 ALU.add), "logit")
            for t in range(TT):
                link(V.max(top[:, t, :], lg[:, t, :]))
                link(V.max_index(topi[:, t, :], top[:, t, :], lg[:, t, :]))
                tsc(topw[:, t, 4:5], top[:, t, 0:1], -1.0, ALU.mult)
            link(V.tensor_copy(topf[:, :, :], topi[:, :, :]), top_ready, 1)
            dve.wait_ge(topexp_done, 2)
            for t in range(TT):
                link(V.reciprocal(topw[:, t, 6:7], topw[:, t, 5:6]))
                tsc(topw[:, t, 0:TOPK], topw[:, t, 0:TOPK], topw[:, t, 6:7], ALU.mult)
                tsc(comb[:, t, :], iota_e[:, :], topf[:, t, 0:1], ALU.is_equal, topw[:, t, 0:1], ALU.mult)
                for k in range(1, TOPK):
                    tsc(ctmp[:, :], iota_e[:, :], topf[:, t, k:k + 1], ALU.is_equal, topw[:, t, k:k + 1], ALU.mult)
                    tt(comb[:, t, :], comb[:, t, :], ctmp[:, :], ALU.add)
            link(V.tensor_scalar(chosen[:, :, :], comb[:, :, :], 0.0, None, ALU.is_gt), chosen_ready, 1)
            wait_full(dve, "pos")
            o = bank("pos")
            link(V.scalar_tensor_tensor(posm[:, :, :], o[:, 0:64].rearrange("p (t e) -> p t e", t=TT), 1.0,
                                        chosen[:, :, :], op0=ALU.add, op1=ALU.mult))
            tsc(posm[:, :, :], posm[:, :, :], 1.0, ALU.subtract)
            free(V.tensor_reduce(cmax[:, :], o[:, 64:96], AX.X, ALU.max), "pos")
            link(V.tensor_copy(count[:, :], cmax[:, :]), count_ready, 1)

            def one_hots(e, i):
                for a in range(2):
                    for t in range(TT):
                        ins = V.tensor_scalar(onehot[:, t, SLOTS * a:SLOTS * a + SLOTS], iota2[:, 0:SLOTS],
                                              posm[:, t, bass.ds(e + a, 1)], None, ALU.is_equal)
                ins.then_inc(onehot_ready, 1)

            def weighted(e):
                for a in range(2):
                    for t in range(TT):
                        ins = V.tensor_scalar(onehot_w[:, a, t, :], iota2[:, :], posm[:, t, bass.ds(e + a, 1)],
                                              comb[:, t, bass.ds(e + a, 1)], ALU.is_equal, ALU.mult)
                ins.then_inc(weighted_ready, 1)

            def bias_rows(e, par):
                V.tensor_copy(bias_row[:, par, :], ident[:, bass.ds(e + par, 1)].broadcast_to([P, SLOTS]))\
                    .then_inc(row_ready, 1)

            def activation(eg, par, c, first=False):
                if not first:
                    dve.wait_ge(act_ready, eg + c)
                dve.wait_ge(w1_used, (eg + (c + 1)) * KD)
                h = ps[:, H0:H0 + 2, :].rearrange("p b (n two) -> p b n two", two=2)
                V.tensor_scalar(hid_g, h[:, :, :, 0], LIMIT, None, ALU.min).then_inc(glu_in, 1)
                V.tensor_scalar(hid_l, h[:, :, :, 1], LIMIT, -LIMIT, ALU.min, ALU.max).then_inc(hid_free, 1)
                dve.wait_ge(hid_free, eg + (c + 1))
                V.scalar_tensor_tensor(hid_l, hid_l, 1.0, hid_g, op0=ALU.add, op1=ALU.mult).then_inc(moe_dve, 1)
                dve.wait_ge(moe_dve, eg + (c + 1))
                dve.wait_ge(sig_done, eg + (c + 1))
                V.tensor_tensor(act_sb[:, par], hid_l, hid_s, ALU.mult).then_inc(act_ready, 1)

            def moe(p, first_pass):
                eg0 = p * EXPERTS
                if not first_pass:
                    V.tensor_scalar(posm[:, :, :], posm[:, :, :], float(SLOTS), None, ALU.subtract)\
                        .then_inc(pass_step, 1)
                    dve.wait_ge(pass_step, p)
                    dve.wait_ge(gather_full, p * 32)
                one_hots(0, p * 16)

                def pair(e, i, first=False, last=False):
                    if not (first and first_pass):
                        dve.wait_ge(w1_used, i * 16)
                    bias_rows(e, 0)
                    bias_rows(e, 1)
                    if not (first and first_pass):
                        dve.wait_ge(scT_full, i)
                    weighted(e)
                    if not last:
                        dve.wait_ge(gather_full, i * 2 + 2)
                        one_hots(e + 2, i + 1)
                    activation(2 * i, 0, 0, first and first_pass)
                    activation(2 * i, 1, 1)

                pair(0, p * 16, first=True)
                with dve.Fori(1, 15) as i:
                    pair(i * 2, i + p * 16)
                pair(30, p * 16 + 15, last=True)

            moe(0, True)
            dve.wait_ge(count_ready, 1)
            most = dve.value_load(count[0:1, 0:1], min_val=0, max_val=SEQ)
            with dve.Fori(1, PASSES) as p:
                with dve.If(most > p * SLOTS):
                    moe(p, False)
            dve.wait_ge(acc_full, 1)
            for t in range(TT):
                V.tensor_tensor(xres[:, t, :], ps[:, 2 * t:2 * t + 2, :].rearrange("p a b -> p (a b)"),
                                xres[:, t, :], ALU.add).then_inc(out_ready, 1)


_NAMES = ['x', 'mem', 'positions', 'attn_norm_g', 'mem_norm_g', 'w_in', 'b_gate',
          'ssm_log_dt', 'ssm_a_re', 'ssm_a_im', 'ssm_b_re', 'ssm_b_im', 'ssm_c_re', 'ssm_c_im', 'ssm_d',
          'w_glu_v', 'w_glu_g', 'swa_q_gain', 'swa_k_gain', 'swa_sinks',
          'w_mem_kv', 'mem_q_gain', 'mem_k_gain',
          'w_br_ssm', 'w_br_swa', 'w_br_mem', 'w_out',
          'ffn_norm_g', 'w_router', 'b_router', 'w_mlp1', 'b_mlp1', 'w_mlp2', 'b_mlp2']


def kernel(**inputs):
    import concourse.bacc as bacc
    from concourse.bass_utils import run_bass_kernel_spmd

    nc = bacc.Bacc("TRN2", target_bir_lowering=False, num_devices=1)
    arrays, args = {}, []
    for name in _NAMES:
        a = np.ascontiguousarray(np.asarray(inputs[name])[0])
        arrays["in_" + name] = a
        args.append(nc.dram_tensor("in_" + name, a.shape, mybir.dt.from_np(a.dtype), kind="ExternalInput").ap())
    args.append(nc.dram_tensor("layer_out", (SEQ, D), F32, kind="ExternalOutput").ap())
    hybrid_layer(nc, *args)
    r = run_bass_kernel_spmd(nc, [arrays], core_ids=[0])
    return r.results[0]["layer_out"].reshape(1, SEQ, D)
```
